# Optimizing a Trainium2 kernel written in Bass

```python
import jax, jax.numpy as jnp
from jax import lax
import numpy as np

D_MODEL = 1024
BATCH = 1
SEQ = 256
DEPTH = 2

N_GMLP_GROUPS = 8
GMLP_GROUP_DIM = 64
GMLP_WIDTH = N_GMLP_GROUPS * GMLP_GROUP_DIM
CHUNK = 128
N_SB_HEADS = 8
SB_HEAD_DIM = 64
SB_WIDTH = N_SB_HEADS * SB_HEAD_DIM
SB_BLOCK = 128
EVEN_IN_WIDTH = 2 * GMLP_WIDTH + 3 * SB_WIDTH
EVEN_MIX_WIDTH = GMLP_WIDTH + SB_WIDTH
CONV_WIDTH = D_MODEL
CONV_K = 3
N_GROUPS = 4
EXPERTS_PER_GROUP = 8
N_EXPERTS = N_GROUPS * EXPERTS_PER_GROUP
EXPERT_TOP_K = 2
EXPERT_FF = 512
EPS = 1e-6
N_EVEN = (DEPTH + 1) // 2
N_ODD = DEPTH // 2

kernel_name = "hybrid_gmlp_stickbreak_shortconv_hmoe"

def rms_norm(x, gain):
    xf = x.astype(jnp.float32)
    y = xf * lax.rsqrt(jnp.mean(xf * xf, axis=-1, keepdims=True) + EPS)
    return (y * gain.astype(jnp.float32)).astype(x.dtype)

def chunked_spatial_gating(u, v, w_s, b_s, v_gain):
    b, s, g, d = v.shape
    v = rms_norm(v, v_gain)
    causal = jnp.tril(jnp.ones((CHUNK, CHUNK), dtype=bool))
    w = jnp.where(causal[None], w_s, jnp.zeros_like(w_s)).astype(v.dtype)
    vc = v.reshape(b, s // CHUNK, CHUNK, g, d)
    mixed = jnp.einsum('gts,bnsgd->bntgd', w, vc) + b_s.T.astype(v.dtype)[None, None, :, :, None]
    return u * mixed.reshape(b, s, g, d)

def stick_breaking_attention(q, k, v):
    b, s, h, d = q.shape
    nb = s // SB_BLOCK
    scale = d ** -0.5
    qb = q.reshape(b, nb, SB_BLOCK, h, d).transpose(1, 0, 2, 3, 4)
    kpos = jnp.arange(s)

    def block(args):
        qi, i = args
        z = jnp.einsum('bthd,bshd->bhts', qi, k).astype(jnp.float32) * scale
        qpos = i * SB_BLOCK + jnp.arange(SB_BLOCK)
        causal = kpos[None, :] < qpos[:, None]
        log_beta = jax.nn.log_sigmoid(z)
        log_keep = jnp.where(causal, jax.nn.log_sigmoid(-z), 0.0)
        suffix = lax.cumsum(log_keep, axis=3, reverse=True) - log_keep
        a = jnp.where(causal, jnp.exp(log_beta + suffix), 0.0)
        return jnp.einsum('bhts,bshd->bthd', a.astype(v.dtype), v)

    out = lax.map(block, (qb, jnp.arange(nb)))
    return out.transpose(1, 0, 2, 3, 4).reshape(b, s, h, d)

def short_conv_mixer(p, conv_w):
    gate_b, gate_c, h = jnp.split(p, 3, axis=-1)
    y = gate_c * h
    conv = lax.conv_general_dilated(
        y, conv_w.astype(y.dtype)[:, None, :],
        window_strides=(1,), padding=[(CONV_K - 1, 0)],
        dimension_numbers=('NWC', 'WIO', 'NWC'),
        feature_group_count=CONV_WIDTH)
    return gate_b * conv

def hierarchical_moe(x, w_router_group, w_router_expert, w_gate, w_up, w_down):
    b, s, d = x.shape
    t = x.reshape(-1, d)
    group_prob = jax.nn.softmax((t @ w_router_group).astype(jnp.float32), axis=-1)
    top_gp, top_g = lax.top_k(group_prob, 1)
    top_gp, top_g = top_gp[:, 0], top_g[:, 0]
    expert_logits = jnp.einsum('td,gde->tge', t, w_router_expert).astype(jnp.float32)
    sel_logits = jnp.take_along_axis(expert_logits, top_g[:, None, None], axis=1)[:, 0]
    top_el, top_e = lax.top_k(sel_logits, EXPERT_TOP_K)
    top_ep = jax.nn.softmax(top_el, axis=-1)
    expert_idx = top_g[:, None] * EXPERTS_PER_GROUP + top_e
    weights = top_gp[:, None] * top_ep
    combine = jnp.sum(jax.nn.one_hot(expert_idx, N_EXPERTS, dtype=jnp.float32) * weights[..., None], axis=1)
    combine = combine.astype(t.dtype)
    out = jnp.zeros_like(t)
    for e in range(N_EXPERTS):
        h = jax.nn.silu(t @ w_gate[e]) * (t @ w_up[e])
        out = out + combine[:, e:e + 1] * (h @ w_down[e])
    return out.reshape(b, s, d)

def setup_inputs(seed: int = 0) -> dict:
    key = jax.random.key(seed)
    ks = jax.random.split(key, 18)
    f32 = jnp.float32
    nrm = lambda k, shape, scale: jax.random.normal(k, shape, f32) * scale
    return {
        "x": jax.random.normal(ks[0], (BATCH, SEQ, D_MODEL), f32),
        "even_w_in": nrm(ks[1], (N_EVEN, D_MODEL, EVEN_IN_WIDTH), D_MODEL ** -0.5),
        "even_w_out": nrm(ks[2], (N_EVEN, EVEN_MIX_WIDTH, D_MODEL), EVEN_MIX_WIDTH ** -0.5),
        "gmlp_w_s": nrm(ks[3], (N_EVEN, N_GMLP_GROUPS, CHUNK, CHUNK), CHUNK ** -0.5),
        "gmlp_b_s": 1.0 + nrm(ks[4], (N_EVEN, N_GMLP_GROUPS, CHUNK), 0.1),
        "gmlp_v_gain": 1.0 + nrm(ks[5], (N_EVEN, N_GMLP_GROUPS, GMLP_GROUP_DIM), 0.05),
        "odd_w_in": nrm(ks[6], (N_ODD, D_MODEL, 3 * CONV_WIDTH), D_MODEL ** -0.5),
        "odd_conv_w": nrm(ks[7], (N_ODD, CONV_K, CONV_WIDTH), CONV_K ** -0.5),
        "odd_w_out": nrm(ks[8], (N_ODD, CONV_WIDTH, D_MODEL), CONV_WIDTH ** -0.5),
        "norm_mix": 1.0 + nrm(ks[9], (DEPTH, D_MODEL), 0.05),
        "norm_ffn": 1.0 + nrm(ks[10], (DEPTH, D_MODEL), 0.05),
        "router_group": nrm(ks[11], (DEPTH, D_MODEL, N_GROUPS), D_MODEL ** -0.5),
        "router_expert": nrm(ks[12], (DEPTH, N_GROUPS, D_MODEL, EXPERTS_PER_GROUP), D_MODEL ** -0.5),
        "w_gate": nrm(ks[13], (DEPTH, N_EXPERTS, D_MODEL, EXPERT_FF), D_MODEL ** -0.5),
        "w_up": nrm(ks[14], (DEPTH, N_EXPERTS, D_MODEL, EXPERT_FF), D_MODEL ** -0.5),
        "w_down": nrm(ks[15], (DEPTH, N_EXPERTS, EXPERT_FF, D_MODEL), EXPERT_FF ** -0.5),
        "norm_final": 1.0 + nrm(ks[16], (D_MODEL,), 0.05),
    }

def reference(x, even_w_in, even_w_out, gmlp_w_s, gmlp_b_s, gmlp_v_gain,
              odd_w_in, odd_conv_w, odd_w_out, norm_mix, norm_ffn,
              router_group, router_expert, w_gate, w_up, w_down, norm_final):
    b, s, _ = x.shape
    for l in range(DEPTH):
        h = rms_norm(x, norm_mix[l])
        i = l // 2
        if l % 2 == 0:
            p = h @ even_w_in[i]
            u, v, q, k, vv = jnp.split(
                p, [GMLP_WIDTH, 2 * GMLP_WIDTH, 2 * GMLP_WIDTH + SB_WIDTH,
                    2 * GMLP_WIDTH + 2 * SB_WIDTH], axis=-1)
            u = jax.nn.gelu(u, approximate=False).reshape(b, s, N_GMLP_GROUPS, GMLP_GROUP_DIM)
            v = jax.nn.gelu(v, approximate=False).reshape(b, s, N_GMLP_GROUPS, GMLP_GROUP_DIM)
            a_out = chunked_spatial_gating(u, v, gmlp_w_s[i], gmlp_b_s[i], gmlp_v_gain[i])
            heads = lambda t: t.reshape(b, s, N_SB_HEADS, SB_HEAD_DIM)
            b_out = stick_breaking_attention(heads(q), heads(k), heads(vv))
            mix = jnp.concatenate([a_out.reshape(b, s, GMLP_WIDTH),
                                   b_out.reshape(b, s, SB_WIDTH)], axis=-1) @ even_w_out[i]
        else:
            mix = short_conv_mixer(h @ odd_w_in[i], odd_conv_w[i]) @ odd_w_out[i]
        x = x + mix
        x = x + hierarchical_moe(rms_norm(x, norm_ffn[l]), router_group[l], router_expert[l],
                                 w_gate[l], w_up[l], w_down[l])
    return rms_norm(x, norm_final)


_drawn_inputs = setup_inputs


def setup_inputs(seed=0):
    import zlib

    import numpy as np

    out = dict(_drawn_inputs(seed))
    spreads = {}
    factors = {}
    for name, (base, spread) in spreads.items():
        noise = np.random.default_rng([zlib.crc32(name.encode()), seed]).standard_normal(out[name].shape)
        drawn = base * np.exp(spread * noise) if base else spread * noise
        out[name] = __import__('jax').numpy.asarray(drawn.astype(out[name].dtype))
    for name, factor in factors.items():
        out[name] = (out[name] * factor).astype(out[name].dtype)
    return out
```

```python
from contextlib import ExitStack, contextmanager

import concourse.bass as bass
from concourse import mybir

F32 = mybir.dt.float32
I32 = mybir.dt.int32
ALU = mybir.AluOpType
ACT = mybir.ActivationFunctionType
AX_X = mybir.AxisListType.X

P = 128
D = 1024
S = 256
TT = S // P
K = D // P
HD = 64
NH = 8
W1 = NH * HD
G = 4
EG = 8
NE = G * EG
FF = 512
CAP = 32
NP = P // CAP
FP = FF // NP
DP = D // NP
CONV = 3
EPS = 1e-6
BIG = 1e30
LINEAR = 40.0
RING = 9
SLOT = 4096
TRI = 3
TURNS = (NE - 1) // TRI
REST = NE - TURNS * TRI
TRIS = TURNS + 1
CHUNKS = 2
KC = K // CHUNKS
MAX_MORE = (S - 1) // CAP
MAX_TOTAL = 2 * S // CAP

L_EVEN = 0
L_MOE = [7, 7 + 3 * NE + 8]
L_ODD = 7 + 3 * NE
L_GAIN = L_MOE[1] + 3 * NE


def trunk(nc, x_in, even_w_in, even_w_out, gmlp_w_s, gmlp_b_s, gmlp_v_gain, odd_w_in, odd_conv_w,
          odd_w_out, norm_mix, norm_ffn, router_group, router_expert, w_gate, w_up, w_down,
          norm_final, out):
    with ExitStack() as ctx:
        def sb(name, cols, dt=F32, rows=P):
            return ctx.enter_context(nc.sbuf_tensor(name, [rows, cols], dt))

        def sem(name):
            return ctx.enter_context(nc.semaphore(name))

        ring = sb("ring", RING * SLOT)
        x = sb("x", TT * D)[:, :].rearrange("p (t d) -> p t d", t=TT)
        hn_flat = sb("hn", TT * D)
        hn = hn_flat[:, :].rearrange("p (t k q) -> p t k q", t=TT, k=K)
        mixT = hn_flat[:, :].rearrange("p (j t) -> p j t", j=K)
        fin = hn_flat[:, :].rearrange("p (t d) -> p t d", t=TT)
        scr = sb("scr", 4096)
        hT = scr[:, 0:2048].rearrange("p (k t) -> p k t", k=K)
        att = [scr[:, 2048 + 384 * i:2048 + 384 * (i + 1)] for i in range(4)]
        vsq = scr[:, 3584:4096]
        xb = scr[:, :]
        m = sb("m", 5120)
        uT = m[:, 0:1024].rearrange("p (j t) -> p j t", j=4)
        v = m[:, 1024:2048].rearrange("p (t c) -> p t c", t=TT)
        qT = m[:, 2048:3072].rearrange("p (j t) -> p j t", j=4)
        kT = m[:, 3072:4096].rearrange("p (j t) -> p j t", j=4)
        vv = m[:, 4096:5120].rearrange("p (t c) -> p t c", t=TT)
        ws = m[:, 2048:3072].rearrange("p (g s) -> p g s", g=NH)
        bs = m[:, 3072:3584].rearrange("p (j t) -> p j t", j=4)
        cbuf = m[:, 0:1024].rearrange("p (j t) -> p j t", j=4)
        PAD = CONV - 1
        ybuf = m[:, 1024:1024 + 4 * (S + PAD)].rearrange("p (j t) -> p j t", j=4)
        cv = m[:, 2080:3104].rearrange("p (j t) -> p j t", j=4)
        used_m = [0]

        def temp(cols):
            at = used_m[0]
            used_m[0] += cols
            assert used_m[0] <= 5120
            return m[:, at:at + cols]

        xg = temp(K * TRI * CAP).rearrange("p (k c) -> p k c", k=K)
        sel = temp(TT * TRI * CAP).rearrange("p (t c) -> p t c", t=TT)
        wsel = temp(TT * P).rearrange("p (t c) -> p t c", t=TT)
        cmb = temp(TT * P)
        sg = temp(FP)
        hh = temp(FP)
        hhT = temp(P)
        yy = temp(DP)
        lg = temp(TT * (G + NE)).rearrange("p (t e) -> p t e", t=TT)
        ml = temp(TT * NE).rearrange("p (t e) -> p t e", t=TT)
        ml2 = temp(TT * NE).rearrange("p (t e) -> p t e", t=TT)
        eq = temp(TT * NE).rearrange("p (t e) -> p t e", t=TT)
        oh1 = temp(TT * NE).rearrange("p (t e) -> p t e", t=TT)
        oh2 = temp(TT * NE).rearrange("p (t e) -> p t e", t=TT)
        chosen = temp(TT * NE).rearrange("p (t e) -> p t e", t=TT)
        gs = temp(TT * G).rearrange("p (t g) -> p t g", t=TT)
        geq = temp(TT * G).rearrange("p (t g) -> p t g", t=TT)
        (gmax, gsum, gidx, m1, m2, i1, e2, den, wt1, wt2) = (temp(TT) for _ in range(10))
        over = temp(NE * MAX_MORE).rearrange("p (e r) -> p e r", e=NE)
        more = temp(NE)
        HALO = NE // 2
        sums = [temp(HALO + NE) for _ in range(2)]

        ident, below, upto, nlin, ones, nones, diag = (sb(n, P) for n in (
            "ident", "below", "upto", "nlin", "ones", "nones", "diag"))
        count = sb("count", S)
        rank32 = sb("rank32", NE)
        eps = sb("eps", 1)
        gains = sb("gains", 4 * K)[:, :].rearrange("p (n k) -> p n k", n=4)
        rows = sb("rows", P, rows=28)
        colsT = sb("colsT", 28)
        rgraw = sb("rgraw", 2 * K * G)[:, :].rearrange("p (l k g) -> p l k g", l=2, k=K)
        reraw = sb("reraw", 2 * K * NE)[:, :].rearrange("p (l g k e) -> p l g k e", l=2, g=G, k=K)
        rw = sb("rw", 2 * K * (G + NE))[:, :].rearrange("p (l k e) -> p l k e", l=2, k=K)
        ssq = sb("ssq", TT)
        rstd = sb("rstd", TT)
        ssv = sb("ssv", TT * NH)
        rsv = sb("rsv", TT * NH)
        pos = sb("pos", TT * (NE + 1))
        cw = sb("cw", TT * (NE + 1))
        extra = sb("extra", 2 * NE + 1, I32)
        psum = ctx.enter_context(nc.psum_tensor("psum", [P, 8, 512], F32))
        bank = [psum[:, i, :] for i in range(8)]
        GU, YB, BA, BB = bank[4], bank[5], bank[6], bank[7]

        landed = [sem(f"landed{i}") for i in range(RING)]
        gate_used, out_half = sem("gate_used"), sem("out_half")
        x_loaded = [sem(f"x_loaded{t}") for t in range(TT)]
        smalls_loaded = [sem(f"smalls_loaded{i}") for i in range(7)]
        final_ready = sem("final_ready")
        ws_loaded, bs_loaded, out_stored = sem("ws_loaded"), sem("bs_loaded"), sem("out_stored")
        pool_step, consts_ready = sem("pool_step"), sem("consts_ready")
        router_ready = sem("router_ready")
        dve_step, act_step = sem("dve_step"), sem("act_step")
        cols_turned, cols_ready = sem("cols_turned"), sem("cols_ready")
        x_ready = sem("x_ready")
        std_ready, rstd_ready = sem("std_ready"), sem("rstd_ready")
        hn_dve, hn_act = sem("hn_dve"), sem("hn_act")
        turned, hT_dve, hT_act = sem("turned"), sem("hT_dve"), sem("hT_act")
        q_ready, q_taken = sem("q_ready"), sem("q_taken")
        k_ready, k_taken = sem("k_ready"), sem("k_taken")
        vv_ready, vv_taken = sem("vv_ready"), sem("vv_taken")
        v_ready, v_gelu = sem("v_ready"), sem("v_gelu")
        u_ready, u_gelu = sem("u_ready"), sem("u_gelu")
        ssv_ready, stdv_ready, vn_ready = sem("ssv_ready"), sem("stdv_ready"), sem("vn_ready")
        z_ready, clip_ready, ln_ready, sp_ready = sem("z_ready"), sem("clip_ready"), sem("ln_ready"), sem("sp_ready")
        s_ready, low_ready, a_ready = sem("s_ready"), sem("low_ready"), sem("a_ready")
        av_ready, av_taken = sem("av_ready"), sem("av_taken")
        ws_turned, ws_ready = sem("ws_turned"), sem("ws_ready")
        gate_ready, gate_taken = sem("gate_ready"), sem("gate_taken")
        o_ready = sem("o_ready")
        pc_ready, pc_taken = sem("pc_ready"), sem("pc_taken")
        ph_ready, y_made = sem("ph_ready"), sem("y_made")
        pb_ready, zc_ready = sem("pb_ready"), sem("zc_ready")
        logits_ready, exps_ready, exp2_ready, d_ready = sem("logits_ready"), sem("exps_ready"), sem("exp2_ready"), sem("d_ready")
        gsub_ready, chosen_ready, rank_ready, extra_ready = sem("gsub_ready"), sem("chosen_ready"), sem("rank_ready"), sem("extra_ready")
        sel_ready, gathered, xg_ready = sem("sel_ready"), sem("gathered"), sem("xg_ready")
        wsel_ready, cmb_turned, cmb_ready = sem("wsel_ready"), sem("cmb_turned"), sem("cmb_ready")
        gu_ready, silu_ready, h_ready = sem("gu_ready"), sem("silu_ready"), sem("h_ready")
        h_turned, hhT_ready, y_ready, yy_ready = sem("h_turned"), sem("hhT_ready"), sem("y_ready"), sem("yy_ready")
        xs = [{n: sem(f"x{n}{l}") for n in (
            "landed", "gate", "sel", "gathered", "xg", "gu", "silu", "h", "turned", "evac", "y", "yy", "done")}
            for l in range(2)]

        block = ctx.enter_context(nc.Block())

        def slot(n):
            return ring[:, (n % RING) * SLOT:(n % RING + 1) * SLOT]

        def wide(n):
            return slot(n).rearrange("p (k f) -> p k f", k=K)

        def tall(n):
            return slot(n).rearrange("p (j d) -> p j d", j=4)

        def wait_landed(eng, n, turns=0):
            eng.wait_ge(landed[n % RING], (turns + (n // RING + 1)) * 16)

        @contextmanager
        def further(eng):
            total = eng.value_load(extra[0:1, 2 * NE:2 * NE + 1], min_val=0, max_val=MAX_TOTAL)

            @contextmanager
            def each():
                with eng.Fori(0, NE) as e:
                    blocks = eng.value_load(extra[0:1, bass.ds(e, 1)], min_val=0, max_val=MAX_MORE)
                    before = eng.value_load(extra[0:1, bass.ds(e + NE, 1)], min_val=0, max_val=MAX_TOTAL)
                    with eng.If(blocks > 0):
                        with eng.Fori(0, blocks) as r:
                            yield e, r, before + r + 1
                    eng.nop()

            each.total = total
            with eng.If(total > 0):
                yield each
            eng.nop()

        def after(l, e):
            return e + (NE * l + 1)

        def after_z(l, e):
            return e + ((NE + 1) * l + 2)

        def after_chunk(l, T, q):
            return T * CHUNKS + (CHUNKS * TRIS * l + q + 1)

        @block.sync
        def _(sp):
            def used_up(n):
                for l in range(2):
                    if L_MOE[l] <= n < L_MOE[l] + 3 * NE:
                        e, mat = divmod(n - L_MOE[l], 3)
                        return (gate_used, gu_ready, y_ready)[mat], after(l, e)
                if n < L_MOE[0]:
                    return ((q_ready, 2), (k_ready, 2), (vv_ready, 2), (v_ready, 2), (u_ready, 2),
                            (out_half, 1), (o_ready, TT))[n - L_EVEN]
                return ((pc_ready, 2), (ph_ready, 2), (pb_ready, 2), (pc_ready, 4), (ph_ready, 4), (pb_ready, 4),
                        (out_half, 2), (o_ready, 2 * TT + 1))[n - L_ODD]

            def load(n, src, dst):
                sp.dma_start(dst, src).then_inc(landed[n % RING], 16)

            def fill(n, src, dst):
                if n >= RING:
                    sp.wait_ge(*used_up(n - RING))
                load(n, src, dst)

            def cols(w, c):
                return w[:, c * 512:(c + 1) * 512].rearrange("(p k) f -> p k f", k=K)

            def outrows(w, r):
                return w[r * 512:(r + 1) * 512, :].rearrange("(j p) d -> p j d", p=P)

            def expert(l, b, i):
                e = b * TRI + i
                for mat, (w, used) in enumerate(((w_gate, gate_used), (w_up, gu_ready), (w_down, y_ready))):
                    n = L_MOE[l] + 3 * i + mat
                    src = w[l, e].rearrange("(j p) d -> p j d", p=P) if mat == 2 else \
                        w[l, e].rearrange("(p k) f -> p k f", k=K)
                    dst = tall(n) if mat == 2 else wide(n)
                    if isinstance(b, int):
                        fill(n + b * RING, src, dst)
                    else:
                        sp.wait_ge(used, after(l, e - TRI))
                        load(n, src, dst)

            def experts(l):
                for i in range(TRI):
                    expert(l, 0, i)
                with sp.Fori(1, TURNS) as b:
                    for i in range(TRI):
                        expert(l, b, i)
                for i in range(REST):
                    expert(l, TURNS, i)
                X = xs[l]
                sp.wait_ge(extra_ready, l + 1)
                with further(sp) as each:
                    with each() as (e, r, n):
                        for mat, w in enumerate((w_gate, w_up, w_down)):
                            sp.wait_ge(X[("done", "gate", "gu")[mat]], n)
                            if mat < 2:
                                src = w[l, e].rearrange("(p k) f -> p k f", k=K)
                                dst = xb.rearrange("p (k f) -> p k f", k=K)
                            else:
                                src = w[l, e].rearrange("(j p) d -> p j d", p=P)
                                dst = xb.rearrange("p (j d) -> p j d", j=4)
                            sp.dma_start(dst, src).then_inc(X["landed"], 16)

            def small_loads():
                sp.dma_start(rows[0:24, :], odd_conv_w[0].rearrange("c (j p) -> (c j) p", p=P)).then_inc(smalls_loaded[2], 16)
                sp.dma_start(rows[24:28, :], gmlp_v_gain[0].rearrange("(j a) d -> j (a d)", a=2)).then_inc(smalls_loaded[3], 16)
                for l in range(2):
                    sp.dma_start(rgraw[:, l], router_group[l].rearrange("(p k) g -> p k g", k=K)).then_inc(smalls_loaded[5], 16)
                    sp.dma_start(reraw[:, l], router_expert[l].rearrange("g (p k) e -> p g k e", k=K)).then_inc(smalls_loaded[6], 16)

            for t in range(TT):
                sp.dma_start(x[:, t, :], x_in[0, t * P:(t + 1) * P, :]).then_inc(x_loaded[t], 16)
            sp.dma_start(gains[:, 0:4:2, :], norm_mix.rearrange("n (p k) -> p n k", k=K)).then_inc(smalls_loaded[0], 16)
            sp.dma_start(gains[:, 1:4:2, :], norm_ffn.rearrange("n (p k) -> p n k", k=K)).then_inc(smalls_loaded[1], 16)
            for n, c in enumerate((2, 3, 4, 1, 0)):
                fill(L_EVEN + n, cols(even_w_in[0], c), wide(L_EVEN + n))
                if n == 0:
                    small_loads()
            for r in range(2):
                fill(L_EVEN + 5 + r, outrows(even_w_out[0], r), tall(L_EVEN + 5 + r))
            experts(0)
            for n, c in enumerate((2, 4, 0, 3, 5, 1)):
                fill(L_ODD + n, cols(odd_w_in[0], c), wide(L_ODD + n))
            for r in range(2):
                fill(L_ODD + 6 + r, outrows(odd_w_out[0], r), tall(L_ODD + 6 + r))
            experts(1)
            fill(L_GAIN, norm_final.partition_broadcast(P), slot(L_GAIN)[:, 0:D])
            for t in range(TT):
                sp.wait_ge(final_ready, t + 1)
                sp.dma_start(out[0, t * P:(t + 1) * P, :], fin[:, t, :]).then_inc(out_stored, 16)
            sp.wait_ge(out_stored, 16 * TT)

        @block.gpsimd
        def _(pool):
            steps = [0]

            def link(ins):
                steps[0] += 1
                ins.then_inc(pool_step, 1)
                pool.wait_ge(pool_step, steps[0])

            def ramp(t, base, step, chan, op, fill):
                link(pool.affine_select(out=t[:, :], in_=t[:, :], compare_op=op, fill=fill, base=base,
                                        pattern=[[step, P]], channel_multiplier=chan))

            pool.memset(eps[:, :], EPS)
            pool.memset(ones[:, :], 1.0)
            pool.memset(nones[:, :], -1.0)
            pool.memset(nlin[:, :], -1.0)
            pool.memset(ident[:, :], 0.0)
            pool.memset(below[:, :], 1.0)
            pool.memset(upto[:, :], 1.0)
            pool.memset(diag[:, :], 0.0)
            link(pool.memset(cw[:, :], 0.0))
            ramp(ident, 0, -1, 1, ALU.not_equal, 1.0)
            ramp(below, 0, 1, -1, ALU.is_gt, 0.0)
            ramp(upto, 0, 1, -1, ALU.is_ge, 0.0)
            ramp(diag, 0, 1, -1, ALU.is_gt, -BIG)
            ramp(nlin, 0, -1, 1, ALU.is_ge, 0.0)
            pool.iota(count[:, :], [[1, S]], base=0, channel_multiplier=0, allow_small_or_imprecise_dtypes=True)
            pool.memset(pos[:, :], -1.0)
            link(pool.iota(rank32[:, :], [[-1, NE]], base=NE, channel_multiplier=0,
                           allow_small_or_imprecise_dtypes=True))
            pool.sem_inc(consts_ready, 1)
            for i in (5, 6):
                pool.wait_ge(smalls_loaded[i], 32)
            for l in range(2):
                pool.tensor_copy(rw[:, l, :, 0:G], rgraw[:, l])
                for g in range(G):
                    last = pool.tensor_copy(rw[:, l, :, G + EG * g:G + EG * (g + 1)], reraw[:, l, g])
            last.then_inc(router_ready, 1)

        @block.scalar
        def _(act):
            steps = [0]

            def link(ins):
                steps[0] += 1
                ins.then_inc(act_step, 1)
                act.wait_ge(act_step, steps[0])

            act.wait_ge(consts_ready, 1)

            def squares(n):
                for t in range(TT):
                    if n == 0:
                        act.wait_ge(x_loaded[t], 16)
                    else:
                        act.wait_ge(x_ready, TT * (n - 1) + t + 1)
                    ins = act.activation(m[:, 0:D], x[:, t, :], ACT.Square, accum_out=ssq[:, t:t + 1])
                    if t == 0:
                        link(ins)
                link(ins)
                act.activation(ssq[:, :], ssq[:, :], ACT.Sqrt, bias=eps[:, 0:1], scale=1.0 / D).then_inc(std_ready, 1)

            def norm(n):
                squares(n)
                act.wait_ge(rstd_ready, n + 1)
                act.activation(hn[:, 1].rearrange("p k q -> p q k"), x[:, 1, :].rearrange("p (q k) -> p q k", k=K),
                               ACT.Copy, scale=rstd[:, 1:2]).then_inc(hn_act, 1)
                if n == 0:
                    act.wait_ge(smalls_loaded[0], 16)
                    act.wait_ge(smalls_loaded[1], 16)
                for j in (1, 3):
                    act.wait_ge(turned, 4 * n + j + 1)
                    for kk in range(2):
                        k = 2 * j + kk
                        last = act.activation(hT[:, k, :], bank[4 + j][:, kk * S:(kk + 1) * S], ACT.Copy,
                                              scale=gains[:, n, k:k + 1])
                    last.then_inc(hT_act, 1)

            def even():
                for j in range(2):
                    act.wait_ge(q_ready, j + 1)
                    act.activation(qT[:, 2 * j:2 * j + 2, :], bank[4 + j][:, :].rearrange("p (j t) -> p j t", j=2),
                                   ACT.Copy, scale=HD ** -0.5).then_inc(q_taken, 1)

                def logs(h0):
                    for h in range(h0, h0 + 4):
                        act.wait_ge(clip_ready, h + 1)
                        ins = act.activation(att[h % 4], att[h % 4], ACT.Exp)
                        if h < h0 + 3:
                            link(ins)
                    link(ins)
                    for h in range(h0, h0 + 4):
                        act.activation(att[h % 4], att[h % 4], ACT.Ln, bias=1.0).then_inc(ln_ready, 1)

                def weights(h0):
                    for h in range(h0, h0 + 4):
                        blk = att[h % 4].rearrange("p (b t) -> p b t", b=3)
                        act.wait_ge(low_ready, h + 1)
                        act.activation(blk[:, 0:3:2, :], blk[:, 0:3:2, :], ACT.Exp)
                        act.activation(att[h % 4][:, P:2 * P], bank[h % 4][:, P:2 * P], ACT.Exp).then_inc(a_ready, 1)

                logs(0)
                weights(0)
                for t in range(TT):
                    act.wait_ge(v_ready, t + 1)
                    act.activation(v[:, t, :], bank[6 + t][:, :], ACT.Gelu).then_inc(v_gelu, 1)
                act.wait_ge(ssv_ready, 1)
                act.activation(ssv[:, :], ssv[:, :], ACT.Sqrt, bias=eps[:, 0:1], scale=1.0 / HD).then_inc(stdv_ready, 1)
                act.wait_ge(z_ready, NH)
                act.dma_start(ws, gmlp_w_s[0].rearrange("g t s -> t g s")).then_inc(ws_loaded, 16)
                for a in range(2):
                    src = gmlp_b_s[0].rearrange("(j a) t -> a j t", a=2)[a]
                    act.dma_start(bs[64 * a:64 * a + 64], src.partition_broadcast(HD)).then_inc(bs_loaded, 16)
                logs(4)
                for j in range(2):
                    act.wait_ge(u_ready, j + 1)
                    act.activation(uT[:, 2 * j:2 * j + 2, :], bank[4 + j][:, :].rearrange("p (j t) -> p j t", j=2),
                                   ACT.Gelu).then_inc(u_gelu, 1)
                weights(4)

            def odd():
                for s in range(2):
                    if s:
                        act.wait_ge(y_made, 2)
                    for j in range(2):
                        act.wait_ge(pc_ready, 2 * s + j + 1)
                        act.activation(cbuf[:, 2 * j:2 * j + 2, :], bank[j][:, :].rearrange("p (j t) -> p j t", j=2),
                                       ACT.Copy).then_inc(pc_taken, 1)

            def expert(l, e):
                act.wait_ge(gu_ready, after(l, e))
                act.activation(sg, GU[:, 0:FP], ACT.Silu).then_inc(silu_ready, 1)
                act.wait_ge(cmb_turned, after(l, e))
                act.activation(cmb, BB[:, 0:S], ACT.Copy).then_inc(cmb_ready, 1)
                act.wait_ge(h_turned, after(l, e))
                act.activation(hhT, BA[:, 0:P], ACT.Copy).then_inc(hhT_ready, 1)
                act.wait_ge(y_ready, after(l, e))
                act.activation(yy, YB[:, 0:DP], ACT.Copy).then_inc(yy_ready, 1)

            def moe(l):
                act.wait_ge(gsub_ready, l + 1)
                act.activation(gs, gs, ACT.Exp).then_inc(exps_ready, 1)
                act.wait_ge(d_ready, l + 1)
                act.activation(e2, e2, ACT.Exp).then_inc(exp2_ready, 1)
                with act.Fori(0, TURNS) as b:
                    for i in range(TRI):
                        expert(l, b * TRI + i)
                for i in range(REST):
                    expert(l, TURNS * TRI + i)
                X = xs[l]
                act.wait_ge(extra_ready, l + 1)
                with further(act) as each:
                    with each() as (e, r, n):
                        act.wait_ge(X["gu"], n)
                        act.activation(sg, GU[:, 0:FP], ACT.Silu).then_inc(X["silu"], 1)
                        act.wait_ge(X["turned"], n)
                        act.activation(cmb, BB[:, 0:S], ACT.Copy)
                        act.activation(hhT, BA[:, 0:P], ACT.Copy).then_inc(X["evac"], 1)
                        act.wait_ge(X["y"], n)
                        act.activation(yy, YB[:, 0:DP], ACT.Copy).then_inc(X["yy"], 1)

            norm(0)
            even()
            norm(1)
            moe(0)
            norm(2)
            odd()
            norm(3)
            moe(1)
            squares(4)

        @block.vector
        def _(dve):
            steps = [0]

            def link(ins):
                steps[0] += 1
                ins.then_inc(dve_step, 1)
                dve.wait_ge(dve_step, steps[0])

            def update(n):
                for t in range(TT):
                    dve.wait_ge(o_ready, (TT + 1) * ((n - 1) // 2) + (t + 1 if n % 2 else TT + 1))
                    src = psum[:, 2 * t:2 * t + 2, :] if n % 2 else psum[:, 0:NP, DP * t:DP * (t + 1)]
                    xt = x[:, t, :].rearrange("p (c d) -> p c d", c=2 if n % 2 else NP)
                    dve.tensor_tensor(xt, src, xt, ALU.add).then_inc(x_ready, 1)

            def inverse(n):
                dve.wait_ge(std_ready, n + 1)
                dve.reciprocal(rstd[:, :], ssq[:, :]).then_inc(rstd_ready, 1)
                dve.wait_ge(rstd_ready, n + 1)

            def norm(n):
                if n:
                    update(n)
                inverse(n)
                dve.tensor_scalar(hn[:, 0].rearrange("p k q -> p q k"), x[:, 0, :].rearrange("p (q k) -> p q k", k=K),
                                  rstd[:, 0:1], None, ALU.mult).then_inc(hn_dve, 1)
                if n == 0:
                    dve.wait_ge(smalls_loaded[0], 16)
                    dve.wait_ge(smalls_loaded[1], 16)
                for j in (0, 2):
                    dve.wait_ge(turned, 4 * n + j + 1)
                    dve.tensor_tensor(hT[:, 2 * j:2 * j + 2, :], bank[4 + j][:, :].rearrange("p (k t) -> p k t", k=2),
                                      gains[:, n, 2 * j:2 * j + 2].unsqueeze(2).to_broadcast([P, 2, S]),
                                      ALU.mult).then_inc(hT_dve, 1)

            def even():
                dve.wait_ge(cols_turned, 1)
                dve.tensor_copy(colsT[:, :], bank[0][:, 0:28]).then_inc(cols_ready, 1)
                for j in range(2):
                    dve.wait_ge(k_ready, j + 1)
                    dve.tensor_copy(kT[:, 2 * j:2 * j + 2, :],
                                    bank[6 + j][:, :].rearrange("p (j t) -> p j t", j=2)).then_inc(k_taken, 1)

                def clip(h0):
                    for h in range(h0, h0 + 4):
                        dve.wait_ge(z_ready, h + 1)
                        dve.tensor_scalar(att[h % 4], bank[h % 4][:, 0:384], LINEAR, None, ALU.min).then_inc(clip_ready, 1)

                def softplus(h0):
                    for h in range(h0, h0 + 4):
                        dve.wait_ge(ln_ready, h + 1)
                        link(dve.tensor_tensor(att[h % 4], bank[h % 4][:, 0:384], att[h % 4], ALU.max))
                        blk = att[h % 4].rearrange("p (b t) -> p b t", b=3)[:, 0:3:2, :]
                        dve.tensor_tensor(blk, blk, below[:, :].unsqueeze(1).to_broadcast([P, 2, P]),
                                          ALU.mult).then_inc(sp_ready, 1)

                def lows(h0):
                    for h in range(h0, h0 + 4):
                        dve.wait_ge(s_ready, h + 1)
                        dve.tensor_tensor(att[h % 4].rearrange("p (b t) -> p b t", b=3)[:, 0:3:2, :],
                                          bank[h % 4][:, 0:384].rearrange("p (b t) -> p b t", b=3)[:, 0:3:2, :],
                                          diag[:, :].unsqueeze(1).to_broadcast([P, 2, P]), ALU.min).then_inc(low_ready, 1)

                clip(0)
                softplus(0)
                for t in range(TT):
                    dve.wait_ge(vv_ready, t + 1)
                    dve.tensor_copy(vv[:, t, :], bank[4 + t][:, :]).then_inc(vv_taken, 1)
                lows(0)
                for t in range(TT):
                    dve.wait_ge(v_gelu, t + 1)
                    link(dve.tensor_tensor(vsq, v[:, t, :], v[:, t, :], ALU.mult))
                    ins = dve.tensor_reduce(ssv[:, NH * t:NH * (t + 1)], vsq.rearrange("p (g c) -> p g c", g=NH),
                                            AX_X, ALU.add)
                    ins.then_inc(ssv_ready, 1) if t == TT - 1 else link(ins)
                dve.wait_ge(stdv_ready, 1)
                link(dve.reciprocal(rsv[:, :], ssv[:, :]))
                for t in range(TT):
                    vg = v[:, t, :].rearrange("p (g c) -> p g c", g=NH)
                    dve.tensor_tensor(vg, vg, rsv[:, NH * t:NH * (t + 1)].unsqueeze(2).to_broadcast([P, NH, HD]),
                                      ALU.mult).then_inc(vn_ready, 1)
                dve.wait_ge(av_ready, 1)
                dve.tensor_copy(mixT[:, 4:6, :], bank[6][:, :].rearrange("p (j t) -> p j t", j=2)).then_inc(av_taken, 1)
                clip(4)
                softplus(4)
                lows(4)
                dve.wait_ge(ws_turned, 1)
                for j in range(2):
                    dve.tensor_tensor(ws[:, 4 * j:4 * j + 4, :], bank[6 + j][:, :].rearrange("p (g t) -> p g t", g=4),
                                      upto[:, :].unsqueeze(1).to_broadcast([P, 4, P]), ALU.mult).then_inc(ws_ready, 1)
                dve.wait_ge(bs_loaded, 32)
                dve.wait_ge(u_gelu, 2)
                dve.wait_ge(cols_ready, 1)
                for j in range(4):
                    if j % 2 == 0:
                        dve.wait_ge(gate_ready, j // 2 + 1)
                    g3 = bank[6 + j // 2][:, S * (j % 2):S * (j % 2 + 1)].rearrange("p (c t) -> p c t", c=2)
                    o3 = mixT[:, j, :].rearrange("p (c t) -> p c t", c=2)
                    link(dve.scalar_tensor_tensor(out=o3, in0=g3, scalar=colsT[:, 24 + j:25 + j],
                                                  in1=bs[:, j, :].unsqueeze(1).to_broadcast([P, 2, P]),
                                                  op0=ALU.mult, op1=ALU.add))
                    dve.tensor_tensor(mixT[:, j, :], mixT[:, j, :], uT[:, j, :], ALU.mult).then_inc(gate_taken, 1)
                dve.wait_ge(av_ready, 2)
                dve.tensor_copy(mixT[:, 6:8, :], bank[4][:, :].rearrange("p (j t) -> p j t", j=2)).then_inc(av_taken, 1)

            def odd():
                link(dve.memset(ybuf[:, :, 0:PAD], 0.0))
                for s in range(2):
                    for j in range(2):
                        dve.wait_ge(ph_ready, 2 * s + j + 1)
                        dve.wait_ge(pc_taken, 2 * s + j + 1)
                        dve.tensor_tensor(ybuf[:, 2 * j:2 * j + 2, PAD:], bank[2 + j][:, :].rearrange("p (j t) -> p j t", j=2),
                                          cbuf[:, 2 * j:2 * j + 2, :], ALU.mult).then_inc(y_made, 1)
                    dve.wait_ge(y_made, 2 * s + 2)
                    for tap in range(CONV):
                        for j in range(4):
                            w = colsT[:, tap * K + 4 * s + j:tap * K + 4 * s + j + 1]
                            src = ybuf[:, j, tap:tap + S]
                            if tap == 0:
                                ins = dve.tensor_scalar(cv[:, j, :], src, w, None, ALU.mult)
                            else:
                                ins = dve.scalar_tensor_tensor(out=cv[:, j, :], in0=src, scalar=w, in1=cv[:, j, :],
                                                               op0=ALU.mult, op1=ALU.add)
                        link(ins)
                    for j in range(2):
                        dve.wait_ge(pb_ready, 2 * s + j + 1)
                        dve.tensor_tensor(mixT[:, 4 * s + 2 * j:4 * s + 2 * j + 2, :],
                                          bank[4 + j][:, :].rearrange("p (j t) -> p j t", j=2),
                                          cv[:, 2 * j:2 * j + 2, :], ALU.mult).then_inc(zc_ready, 1)

            def pick(dst, logits, top, scores, best, n):
                link(dve.tensor_reduce(top, logits, AX_X, ALU.max))
                link(dve.tensor_tensor(scores, logits, top.unsqueeze(2).to_broadcast([P, TT, n]), ALU.is_equal))
                ranks = rank32[:, 0:n].unsqueeze(1).to_broadcast([P, TT, n])
                link(dve.tensor_tensor(scores, scores, ranks, ALU.mult))
                link(dve.tensor_reduce(best, scores, AX_X, ALU.max))
                link(dve.tensor_tensor(dst, ranks, best.unsqueeze(2).to_broadcast([P, TT, n]), ALU.is_equal))

            def route(l):
                dve.wait_ge(logits_ready, l + 1)
                link(dve.tensor_copy(lg, bank[4][:, 0:TT * (G + NE)].rearrange("p (t e) -> p t e", t=TT)))
                pick(geq, lg[:, :, 0:G], gmax, gs, gidx, G)
                link(dve.tensor_tensor(gs, lg[:, :, 0:G], gmax.unsqueeze(2).to_broadcast([P, TT, G]), ALU.subtract))
                link(dve.tensor_scalar(geq, geq, BIG, -BIG, ALU.mult, ALU.add))
                dve.sem_inc(gsub_ready, 1)
                for t in range(TT):
                    ins = dve.tensor_tensor(ml[:, t, :].rearrange("p (g e) -> p g e", g=G),
                                            lg[:, t, G:].rearrange("p (g e) -> p g e", g=G),
                                            geq[:, t, :].unsqueeze(2).to_broadcast([P, G, EG]), ALU.add)
                link(ins)
                pick(oh1, ml, m1, eq, i1, NE)
                link(dve.scalar_tensor_tensor(out=ml2, in0=oh1, scalar=-2 * BIG, in1=ml, op0=ALU.mult, op1=ALU.add))
                pick(oh2, ml2, m2, eq, i1, NE)
                dve.tensor_tensor(e2, m2, m1, ALU.subtract).then_inc(d_ready, 1)
                dve.tensor_tensor(chosen, oh1, oh2, ALU.add).then_inc(chosen_ready, 1)
                dve.wait_ge(exps_ready, l + 1)
                link(dve.tensor_reduce(gsum, gs, AX_X, ALU.add))
                dve.wait_ge(exp2_ready, l + 1)
                link(dve.tensor_scalar(den, e2, 1.0, None, ALU.add))
                link(dve.tensor_tensor(den, den, gsum, ALU.mult))
                link(dve.reciprocal(wt1, den))
                link(dve.tensor_tensor(wt2, wt1, e2, ALU.mult))
                link(dve.tensor_tensor(oh1, oh1, wt1.unsqueeze(2).to_broadcast([P, TT, NE]), ALU.mult))
                link(dve.tensor_tensor(oh2, oh2, wt2.unsqueeze(2).to_broadcast([P, TT, NE]), ALU.mult))
                cw3 = cw[:, :].rearrange("p (t e) -> p t e", t=TT)[:, :, 0:NE]
                pos3 = pos[:, :].rearrange("p (t e) -> p t e", t=TT)[:, :, 0:NE]
                link(dve.tensor_tensor(cw3, oh1, oh2, ALU.add))
                dve.wait_ge(rank_ready, l + 1)
                link(dve.scalar_tensor_tensor(out=ml, in0=bank[5][:, 0:TT * NE].rearrange("p (t e) -> p t e", t=TT),
                                              scalar=1.0, in1=chosen, op0=ALU.add, op1=ALU.mult))
                link(dve.tensor_scalar(pos3, ml, -1.0, None, ALU.add))

            def more_blocks(l):
                limits = count[:, CAP:CAP * MAX_MORE + 1:CAP]
                counts = bank[5][:, TT * NE:TT * NE + NE]
                link(dve.tensor_tensor(over, counts.unsqueeze(2).to_broadcast([P, NE, MAX_MORE]),
                                       limits.unsqueeze(1).to_broadcast([P, NE, MAX_MORE]), ALU.is_gt))
                link(dve.tensor_reduce(more, over, AX_X, ALU.add))
                for buf in sums:
                    link(dve.memset(buf, 0.0))
                link(dve.tensor_copy(sums[0][:, HALO:], more))
                step, n = 1, 0
                while step < NE:
                    src, dst = sums[n % 2], sums[(n + 1) % 2]
                    link(dve.tensor_tensor(dst[:, HALO:], src[:, HALO:], src[:, HALO - step:HALO - step + NE], ALU.add))
                    step, n = 2 * step, n + 1
                total = sums[n % 2]
                link(dve.tensor_copy(extra[:, 0:NE], more))
                link(dve.tensor_tensor(extra[:, NE:2 * NE], total[:, HALO:], more, ALU.subtract))
                link(dve.tensor_copy(extra[:, 2 * NE:], total[:, HALO + NE - 1:]))
                dve.sem_inc(extra_ready, 1)

            def at(e, t):
                return (e + t * (NE + 1))

            def select(l, T):
                for i in range(TRI):
                    for t in range(TT):
                        c = at(T * TRI + i, t)
                        last = dve.tensor_scalar(sel[:, t, CAP * i:CAP * (i + 1)], count[:, 0:CAP],
                                                 pos[:, bass.ds(c, 1)], None, ALU.is_equal)
                last.then_inc(sel_ready, 1)

            def weigh(l, e):
                for t in range(TT):
                    c = at(e, t)
                    last = dve.tensor_scalar(wsel[:, t, :].rearrange("p (n c) -> p n c", n=NP),
                                             count[:, 0:CAP].unsqueeze(1).to_broadcast([P, NP, CAP]),
                                             pos[:, bass.ds(c, 1)], cw[:, bass.ds(c, 1)], ALU.is_equal, ALU.mult)
                last.then_inc(wsel_ready, 1)

            def gather(l, T):
                for q in range(CHUNKS):
                    dve.wait_ge(gathered, after_chunk(l, T, q))
                    b = (BA, BB)[q % 2]
                    dve.tensor_tensor(xg[:, KC * q:KC * (q + 1), :],
                                      b[:, 0:KC * TRI * CAP].rearrange("p (k c) -> p k c", k=KC),
                                      gains[:, 2 * l + 1, KC * q:KC * (q + 1)].unsqueeze(2).to_broadcast([P, KC, TRI * CAP]),
                                      ALU.mult).then_inc(xg_ready, 1)

            def expert(l, T, i, last_turn=False, last=False):
                e = T * TRI + i
                if i == 0 and not last_turn:
                    select(l, T + 1)
                dve.wait_ge(gu_ready, after(l, e))
                dve.wait_ge(silu_ready, after(l, e))
                dve.tensor_tensor(hh, GU[:, FP:2 * FP], sg, ALU.mult).then_inc(h_ready, 1)
                if i == TRI - 1:
                    gather(l, T + 1)
                if not last:
                    dve.wait_ge(cmb_turned, after(l, e))
                    weigh(l, e + 1)

            def moe(l):
                dve.memset(cmb, 0.0).then_inc(cmb_ready, 1)
                dve.memset(yy, 0.0).then_inc(yy_ready, 1)
                route(l)
                select(l, 0)
                weigh(l, 0)
                gather(l, 0)
                more_blocks(l)
                with dve.Fori(0, TURNS) as b:
                    for i in range(TRI):
                        expert(l, b, i)
                for i in range(REST):
                    expert(l, TURNS, i, last_turn=True, last=i == REST - 1)
                X = xs[l]
                with further(dve) as each:
                    with each() as (e, r, n):
                        dve.wait_ge(X["done"], n)
                        for t in range(TT):
                            c = at(e, t)
                            ranks = count[:, bass.ds((r + 1) * CAP, CAP)]
                            dve.tensor_scalar(sel[:, t, 0:CAP], ranks, pos[:, bass.ds(c, 1)], None, ALU.is_equal)
                            last = dve.tensor_scalar(wsel[:, t, :].rearrange("p (n c) -> p n c", n=NP),
                                                     ranks.unsqueeze(1).to_broadcast([P, NP, CAP]),
                                                     pos[:, bass.ds(c, 1)], cw[:, bass.ds(c, 1)], ALU.is_equal, ALU.mult)
                        last.then_inc(X["sel"], 1)
                        dve.wait_ge(X["gathered"], n)
                        dve.tensor_tensor(xg[:, :, 0:CAP], BA[:, 0:K * CAP].rearrange("p (k c) -> p k c", k=K),
                                          gains[:, 2 * l + 1, :].unsqueeze(2).to_broadcast([P, K, CAP]),
                                          ALU.mult).then_inc(X["xg"], 1)
                        dve.wait_ge(X["gu"], n)
                        dve.wait_ge(X["silu"], n)
                        dve.tensor_tensor(hh, GU[:, FP:2 * FP], sg, ALU.mult).then_inc(X["h"], 1)
                    dve.wait_ge(X["done"], each.total + 1)
                    dve.tensor_copy(more[:, 0:1], more[:, 0:1])

            dve.wait_ge(consts_ready, 1)
            for t in range(TT):
                dve.wait_ge(x_loaded[t], 16)
            norm(0)
            even()
            norm(1)
            moe(0)
            norm(2)
            odd()
            norm(3)
            moe(1)
            update(4)
            inverse(4)
            wait_landed(dve, L_GAIN)
            for t in range(TT):
                dve.scalar_tensor_tensor(out=fin[:, t, :], in0=x[:, t, :], scalar=rstd[:, t:t + 1],
                                         in1=slot(L_GAIN)[:, 0:D], op0=ALU.mult, op1=ALU.mult).then_inc(final_ready, 1)

        @block.tensor
        def _(pe):
            def norm(n):
                pe.wait_ge(hn_dve, n + 1)
                pe.wait_ge(hn_act, n + 1)
                for j in range(4):
                    for kk in range(2):
                        for t in range(TT):
                            last = pe.transpose(bank[4 + j][:, kk * S + t * P:kk * S + (t + 1) * P],
                                                hn[:, t, 2 * j + kk, :], ident[:, :])
                    last.then_inc(turned, 1)
                pe.wait_ge(hT_dve, 2 * (n + 1))
                pe.wait_ge(hT_act, 2 * (n + 1))

            def channels(n, banks, ready):
                wait_landed(pe, n)
                for c in range(4):
                    for k in range(K):
                        last = pe.matmul(bank[banks[c // 2]][:, (c % 2) * S:(c % 2 + 1) * S],
                                         wide(n)[:, k, P * c:P * (c + 1)], hT[:, k, :], start=k == 0, stop=k == K - 1)
                    if c % 2:
                        last.then_inc(ready, 1)

            def tokens(n, banks, ready):
                wait_landed(pe, n)
                for t in range(TT):
                    for k in range(K):
                        last = pe.matmul(bank[banks[t]][:, :], hT[:, k, P * t:P * (t + 1)], wide(n)[:, k, :],
                                         start=k == 0, stop=k == K - 1)
                    last.then_inc(ready, 1)

            def project_out(n, second_half):
                for r in range(2):
                    wait_landed(pe, n + r)
                    if r == 1:
                        second_half()
                    order = [(j, t) for j in range(4) for t in range(TT)] if r == 0 else \
                        [(j, t) for t in range(TT) for j in range(4)]
                    for j, t in order:
                        for c in range(2):
                            last = pe.matmul(bank[2 * t + c][:, :], mixT[:, 4 * r + j, P * t:P * (t + 1)],
                                             tall(n + r)[:, j, 512 * c:512 * (c + 1)],
                                             start=r == 0 and j == 0, stop=r == 1 and j == 3)
                        if r == 1 and j == 3:
                            last.then_inc(o_ready, 1)
                    if r == 0:
                        last.then_inc(out_half, 1)

            def even():
                L = L_EVEN
                channels(L, (4, 5), q_ready)
                channels(L + 1, (6, 7), k_ready)

                def scores(h):
                    r, c = slice(HD * (h % 2), HD * (h % 2 + 1)), h // 2
                    b = bank[h % 4]
                    pe.matmul(b[:, 0:S], kT[r, c, 0:P], qT[r, c, :], start=True, stop=False, skip_group_check=True)
                    pe.matmul(b[:, S:S + P], kT[r, c, P:S], qT[r, c, P:S], start=False, stop=False,
                              skip_group_check=True).then_inc(z_ready, 1)

                def suffixes(h):
                    a, b = att[h % 4], bank[h % 4]
                    pe.wait_ge(sp_ready, h + 1)
                    pe.matmul(b[:, 0:S], nlin[:, :], a[:, 0:S], start=False, stop=False, skip_group_check=True)
                    pe.matmul(b[:, P:S], nones[:, :], a[:, S:S + P], start=False, stop=False, skip_group_check=True)
                    pe.matmul(b[:, S:S + P], nlin[:, :], a[:, S:S + P], start=False, stop=True,
                              skip_group_check=True).then_inc(s_ready, 1)

                def values(h0, b):
                    for h in range(h0, h0 + 4):
                        pe.wait_ge(a_ready, h + 1)
                        a = att[h % 4]
                        o = bank[b][HD * (h % 2):HD * (h % 2 + 1), S * (h % 4 // 2):S * (h % 4 // 2 + 1)]
                        w = slice(HD * h, HD * (h + 1))
                        pe.matmul(o, vv[:, 0, w], a[:, 0:S], start=True, stop=False, skip_group_check=True)
                        last = pe.matmul(o[:, P:S], vv[:, 1, w], a[:, S:S + P], start=False, stop=True,
                                         skip_group_check=True)
                    last.then_inc(av_ready, 1)

                pe.wait_ge(q_taken, 2)
                pe.wait_ge(k_taken, 2)
                for h in range(4):
                    scores(h)
                tokens(L + 2, (4, 5), vv_ready)
                for h in range(4):
                    suffixes(h)
                tokens(L + 3, (6, 7), v_ready)
                pe.wait_ge(vv_taken, 2)
                pe.wait_ge(v_gelu, 1)
                values(0, 6)
                for h in range(4, 8):
                    scores(h)
                channels(L + 4, (4, 5), u_ready)
                for h in range(4, 8):
                    suffixes(h)
                pe.wait_ge(ws_loaded, 16)
                pe.wait_ge(av_taken, 1)
                pe.wait_ge(v_gelu, 2)
                for g in range(NH):
                    last = pe.transpose(bank[6 + g // 4][:, P * (g % 4):P * (g % 4 + 1)], ws[:, g, :], ident[:, :])
                last.then_inc(ws_turned, 1)
                pe.wait_ge(u_gelu, 1)
                values(4, 4)
                pe.wait_ge(ws_ready, 2)
                pe.wait_ge(vn_ready, 2)
                for j in range(4):
                    for c in range(2):
                        for g in (2 * j, 2 * j + 1):
                            last = pe.matmul(bank[6 + j // 2][HD * (g % 2):HD * (g % 2 + 1),
                                                              S * (j % 2) + P * c:S * (j % 2) + P * (c + 1)],
                                             v[:, c, HD * g:HD * (g + 1)], ws[:, g, :], start=True, stop=True)
                    if j % 2:
                        last.then_inc(gate_ready, 1)
                pe.wait_ge(gate_taken, 4)
                project_out(L + 5, lambda: pe.wait_ge(av_taken, 2))

            def odd():
                L = L_ODD
                for s in range(2):
                    if s:
                        pe.wait_ge(pc_taken, 2)
                    channels(L + 3 * s, (0, 1), pc_ready)
                    if s:
                        pe.wait_ge(y_made, 2)
                    channels(L + 3 * s + 1, (2, 3), ph_ready)
                    if s:
                        pe.wait_ge(zc_ready, 2)
                    channels(L + 3 * s + 2, (4, 5), pb_ready)
                pe.wait_ge(y_made, 4)
                pe.wait_ge(zc_ready, 2)
                project_out(L + 6, lambda: pe.wait_ge(zc_ready, 4))

            def gate_up(w, block_of, lo):
                for k in range(K):
                    for part in range(NP):
                        last = pe.matmul(GU[CAP * part:CAP * (part + 1), lo:lo + FP], block_of(k),
                                         w[:, k, FP * part:FP * (part + 1)], start=k == 0, stop=k == K - 1)
                return last

            def down(w):
                for f in range(NP):
                    for part in range(NP):
                        last = pe.matmul(YB[CAP * part:CAP * (part + 1), 0:DP], hhT[:, CAP * f:CAP * (f + 1)],
                                         w[:, f, DP * part:DP * (part + 1)], start=f == 0, stop=f == NP - 1)
                return last

            def scatter(start=False):
                for t in range(TT):
                    for part in range(NP):
                        r = slice(CAP * part, CAP * (part + 1))
                        last = pe.matmul(bank[part][:, DP * t:DP * (t + 1)], cmb[r, P * t:P * (t + 1)], yy[r, :],
                                         start=start and t == 0, stop=False, skip_group_check=True)
                return last

            def turn_wsel():
                for t in range(TT):
                    last = pe.transpose(BB[:, P * t:P * (t + 1)], wsel[:, t, :], ident[:, :])
                return last

            def turn_h():
                return pe.transpose(BA[:, 0:P], hh, ident[:, :])

            def gather(l, T):
                pe.wait_ge(sel_ready, T + (TRIS * l + 1))
                for q in range(CHUNKS):
                    if q >= 2:
                        pe.wait_ge(xg_ready, after_chunk(l, T, q - 2))
                    b = (BA, BB)[q % 2]
                    for kk in range(KC):
                        for t in range(TT):
                            last = pe.matmul(b[:, kk * TRI * CAP:(kk + 1) * TRI * CAP], hn[:, t, KC * q + kk, :],
                                             sel[:, t, :], start=t == 0, stop=t == TT - 1)
                    last.then_inc(gathered, 1)

            def expert(l, T, i):
                e = T * TRI + i
                n = L_MOE[l] + 3 * i
                for mat in range(2):
                    wait_landed(pe, n + mat, T)
                    last = gate_up(wide(n + mat), lambda k: xg[:, k, CAP * i:CAP * (i + 1)], FP * mat)
                    last.then_inc((gate_used, gu_ready)[mat], 1)
                pe.wait_ge(yy_ready, after_z(l, e - 1))
                pe.wait_ge(cmb_ready, after_z(l, e - 1))
                scatter()
                pe.wait_ge(wsel_ready, after(l, e))
                turn_wsel().then_inc(cmb_turned, 1)
                if i == TRI - 1:
                    pe.wait_ge(cmb_ready, after_z(l, e))
                    gather(l, T + 1)
                    pe.wait_ge(xg_ready, after_chunk(l, T + 1, 0))
                pe.wait_ge(h_ready, after(l, e))
                turn_h().then_inc(h_turned, 1)
                pe.wait_ge(hhT_ready, after(l, e))
                wait_landed(pe, n + 2, T)
                down(tall(n + 2)).then_inc(y_ready, 1)
                if i == TRI - 1:
                    pe.wait_ge(xg_ready, after_chunk(l, T + 1, CHUNKS - 1))

            def moe(l):
                pe.wait_ge(router_ready, 1)
                for t in range(TT):
                    for k in range(K):
                        last = pe.matmul(bank[4][:, (G + NE) * t:(G + NE) * (t + 1)], hT[:, k, P * t:P * (t + 1)],
                                         rw[:, l, k, :], start=k == 0, stop=k == K - 1)
                last.then_inc(logits_ready, 1)
                pe.wait_ge(cmb_ready, after_z(l, -1))
                pe.wait_ge(yy_ready, after_z(l, -1))
                scatter(start=True)
                pe.wait_ge(chosen_ready, l + 1)
                b = bank[5]
                pe.matmul(b[:, 0:NE], below[:, :], chosen[:, 0, :], start=True, stop=True)
                pe.matmul(b[:, NE:2 * NE], ones[:, :], chosen[:, 0, :], start=True, stop=False)
                pe.matmul(b[:, NE:2 * NE], below[:, :], chosen[:, 1, :], start=False, stop=True)
                for t in range(TT):
                    last = pe.matmul(b[:, 2 * NE:3 * NE], ones[:, :], chosen[:, t, :], start=t == 0, stop=t == TT - 1)
                last.then_inc(rank_ready, 1)
                gather(l, 0)
                pe.wait_ge(xg_ready, after_chunk(l, 0, CHUNKS - 1))
                with pe.Fori(0, TURNS) as T:
                    for i in range(TRI):
                        expert(l, T, i)
                for i in range(REST):
                    expert(l, TURNS, i)
                pe.wait_ge(yy_ready, after_z(l, NE - 1))
                pe.wait_ge(cmb_ready, after_z(l, NE - 1))
                X = xs[l]
                scatter().then_inc(o_ready, 1)
                pe.wait_ge(extra_ready, l + 1)
                with further(pe) as each:
                    xw, xt = xb.rearrange("p (k f) -> p k f", k=K), xb.rearrange("p (j d) -> p j d", j=4)
                    pe.sem_inc(X["done"], 1)
                    with each() as (e, r, n):
                        pe.wait_ge(X["sel"], n)
                        for k in range(K):
                            for t in range(TT):
                                last = pe.matmul(BA[:, CAP * k:CAP * (k + 1)], hn[:, t, k, :], sel[:, t, 0:CAP],
                                                 start=t == 0, stop=t == TT - 1)
                        last.then_inc(X["gathered"], 1)
                        pe.wait_ge(X["xg"], n)
                        for mat in range(2):
                            pe.wait_ge(X["landed"], n * 48 - 16 * (2 - mat))
                            gate_up(xw, lambda k: xg[:, k, 0:CAP], FP * mat).then_inc(X[("gate", "gu")[mat]], 1)
                        turn_wsel()
                        pe.wait_ge(X["h"], n)
                        turn_h().then_inc(X["turned"], 1)
                        pe.wait_ge(X["evac"], n)
                        pe.wait_ge(X["landed"], n * 48)
                        down(xt).then_inc(X["y"], 1)
                        pe.wait_ge(X["yy"], n)
                        scatter().then_inc(X["done"], 1)

            pe.wait_ge(consts_ready, 1)
            pe.wait_ge(smalls_loaded[2], 16)
            pe.wait_ge(smalls_loaded[3], 16)
            pe.transpose(bank[0][:, 0:28], rows[:, :], ident[0:28, 0:28]).then_inc(cols_turned, 1)
            norm(0)
            pe.wait_ge(cols_ready, 1)
            even()
            norm(1)
            moe(0)
            norm(2)
            odd()
            norm(3)
            moe(1)


NAMES = ("x", "even_w_in", "even_w_out", "gmlp_w_s", "gmlp_b_s", "gmlp_v_gain", "odd_w_in", "odd_conv_w",
         "odd_w_out", "norm_mix", "norm_ffn", "router_group", "router_expert", "w_gate", "w_up", "w_down",
         "norm_final")


def kernel(**inputs):
    import numpy as np
    import concourse.bacc as bacc
    from concourse.bass_utils import run_bass_kernel_spmd

    nc = bacc.Bacc("TRN2", target_bir_lowering=False, num_devices=1)
    arrays, args = {}, []
    for name in NAMES:
        a = np.ascontiguousarray(inputs[name])
        arrays[f"in_{name}"] = a
        args.append(nc.dram_tensor(f"in_{name}", a.shape, mybir.dt.from_np(a.dtype), kind="ExternalInput").ap())
    args.append(nc.dram_tensor("out", (1, S, D), F32, kind="ExternalOutput").ap())
    trunk(nc, *args)
    return run_bass_kernel_spmd(nc, [arrays], core_ids=[0]).results[0]["out"]
```

```python
from contextlib import ExitStack, contextmanager

import concourse.bass as bass
from concourse import mybir

F32 = mybir.dt.float32
I32 = mybir.dt.int32
ALU = mybir.AluOpType
ACT = mybir.ActivationFunctionType
AX_X = mybir.AxisListType.X

P = 128
D = 1024
S = 256
TT = S // P
K = D // P
HK = K // 2
HD = 64
NH = 8
W1 = NH * HD
G = 4
EG = 8
NE = G * EG
FF = 512
CAP = 32
NP = P // CAP
FP = FF // NP
DP = D // NP
CONV = 3
EPS = 1e-6
BIG = 1e30
LINEAR = 40.0
RING = 9
SLOT = 4096
TRI = 3
TURNS = (NE - 1) // TRI
REST = NE - TURNS * TRI
TRIS = TURNS + 1
CHUNKS = 2
KC = K // CHUNKS
MAX_MORE = (S - 1) // CAP
MAX_TOTAL = 2 * S // CAP

L_EVEN = 0
PER_MOE = 3 * NE - REST
L_MOE = [7, 7 + PER_MOE + 8]
L_ODD = 7 + PER_MOE
L_GAIN = L_MOE[1] + PER_MOE


def trunk(nc, x_in, even_w_in, even_w_out, gmlp_w_s, gmlp_b_s, gmlp_v_gain, odd_w_in, odd_conv_w,
          odd_w_out, norm_mix, norm_ffn, router_group, router_expert, w_gate, w_up, w_down,
          norm_final, out):
    with ExitStack() as ctx:
        def sb(name, cols, dt=F32, rows=P):
            return ctx.enter_context(nc.sbuf_tensor(name, [rows, cols], dt))

        def sem(name):
            return ctx.enter_context(nc.semaphore(name))

        ring = sb("ring", RING * SLOT)
        x_flat = sb("x", TT * D)
        x = x_flat[:, :].rearrange("p (t d) -> p t d", t=TT)
        hn_flat = sb("hn", TT * D)
        hn = hn_flat[:, :].rearrange("p (t k q) -> p t k q", t=TT, k=K)
        mixT = hn_flat[:, :].rearrange("p (j t) -> p j t", j=K)
        fin = hn_flat[:, :].rearrange("p (t d) -> p t d", t=TT)
        scr = sb("scr", 4096)
        hT = scr[:, 0:2048].rearrange("p (k t) -> p k t", k=K)
        att = [scr[:, 2048 + 384 * i:2048 + 384 * (i + 1)] for i in range(4)]
        vsq = scr[:, 3584:4096]
        xb = scr[:, :]
        m = sb("m", 5128)
        early = ((scr[:, 2048:4096], m[:, 3080:5128]),
                 (scr[:, 0:2048], x_flat[:, :]))
        uT = m[:, 0:1024].rearrange("p (j t) -> p j t", j=4)
        v = m[:, 1024:2048].rearrange("p (t c) -> p t c", t=TT)
        qT = m[:, 2048:3072].rearrange("p (j t) -> p j t", j=4)
        kT = m[:, 3072:4096].rearrange("p (j t) -> p j t", j=4)
        vv = m[:, 4096:5120].rearrange("p (t c) -> p t c", t=TT)
        ws = m[:, 2048:3072].rearrange("p (g s) -> p g s", g=NH)
        bs = m[:, 3072:3584].rearrange("p (j t) -> p j t", j=4)
        cbuf = m[:, 0:1024].rearrange("p (j t) -> p j t", j=4)
        PAD = CONV - 1
        ybuf = m[:, 1024:1024 + 4 * (S + PAD)].rearrange("p (j t) -> p j t", j=4)
        cv = m[:, 2056:3080].rearrange("p (j t) -> p j t", j=4)
        used_m = [0]

        def temp(cols):
            at = used_m[0]
            used_m[0] += cols
            assert used_m[0] <= 3080
            return m[:, at:at + cols]

        xg = temp(K * TRI * CAP).rearrange("p (k c) -> p k c", k=K)
        sel = temp(TT * TRI * CAP).rearrange("p (t c) -> p t c", t=TT)
        wsel = temp(TT * P).rearrange("p (t c) -> p t c", t=TT)
        cmb = temp(TT * P)
        sg = temp(FP)
        hh = temp(FP)
        hhT = temp(P)
        yy = temp(DP)
        lg = temp(TT * (G + NE)).rearrange("p (t e) -> p t e", t=TT)
        TAIL = 6
        ml = temp(TT * (NE + TAIL)).rearrange("p (t e) -> p t e", t=TT)
        mr = temp(TT * (NE + TAIL)).rearrange("p (t e) -> p t e", t=TT)
        top8 = temp(TT * 8).rearrange("p (t e) -> p t e", t=TT)
        pair8 = temp(TT * 8).rearrange("p (t e) -> p t e", t=TT)
        chosen = temp(TT * NE).rearrange("p (t e) -> p t e", t=TT)
        ex = temp(TT * NE).rearrange("p (t e) -> p t e", t=TT)
        rk = temp(TT * NE).rearrange("p (t e) -> p t e", t=TT)
        gs = temp(TT * G).rearrange("p (t g) -> p t g", t=TT)
        pen = temp(TT * G).rearrange("p (t g) -> p t g", t=TT)
        (gmax, gneg, gidx, eneg, gsum, den) = (temp(TT) for _ in range(6))
        over = temp(NE * MAX_MORE).rearrange("p (e r) -> p e r", e=NE)
        more = temp(NE)
        HALO = NE // 2
        sums = [temp(HALO + NE) for _ in range(2)]

        ident, below, upto, nlin, ones, nones, diag = (sb(n, P) for n in (
            "ident", "below", "upto", "nlin", "ones", "nones", "diag"))
        count = sb("count", S)
        rank32 = sb("rank32", NE)
        eps = sb("eps", 1)
        gains = sb("gains", 4 * K)[:, :].rearrange("p (n k) -> p n k", n=4)
        rows = sb("rows", P, rows=28)
        colsT = sb("colsT", 28)
        rgraw = sb("rgraw", 2 * K * G)[:, :].rearrange("p (l k g) -> p l k g", l=2, k=K)
        reraw = sb("reraw", 2 * K * NE)[:, :].rearrange("p (l g k e) -> p l g k e", l=2, g=G, k=K)
        rw = sb("rw", 2 * K * (G + NE))[:, :].rearrange("p (l k e) -> p l k e", l=2, k=K)
        junk = sb("junk", 16)
        ssq = sb("ssq", TT)
        rstd = sb("rstd", TT)
        ssv = sb("ssv", TT * NH)
        rsv = sb("rsv", TT * NH)
        pos = sb("pos", TT * (NE + 1))
        cw = sb("cw", TT * (NE + 1))
        extra = sb("extra", 2 * NE + 1, I32)
        psum = ctx.enter_context(nc.psum_tensor("psum", [P, 8, 512], F32))
        bank = [psum[:, i, :] for i in range(8)]
        GU, YB, BA, BB = bank[4], bank[5], bank[6], bank[7]

        landed = [sem(f"landed{i}") for i in range(RING)]
        gate_used, out_half = sem("gate_used"), sem("out_half")
        early_landed = [sem(f"early_landed{i}") for i in range(REST)]
        x_loaded = [sem(f"x_loaded{t}") for t in range(TT)]
        smalls_loaded = [sem(f"smalls_loaded{i}") for i in range(7)]
        final_ready = sem("final_ready")
        ws_loaded, bs_loaded, out_stored = sem("ws_loaded"), sem("bs_loaded"), sem("out_stored")
        pool_step, consts_ready = sem("pool_step"), sem("consts_ready")
        router_ready = sem("router_ready")
        dve_step, act_step = sem("dve_step"), sem("act_step")
        cols_turned, cols_ready = sem("cols_turned"), sem("cols_ready")
        x_ready = sem("x_ready")
        std_ready, rstd_ready = sem("std_ready"), sem("rstd_ready")
        hn_dve, hn_act = sem("hn_dve"), sem("hn_act")
        turned, hT_dve, hT_act = sem("turned"), sem("hT_dve"), sem("hT_act")
        q_ready, q_taken = sem("q_ready"), sem("q_taken")
        k_ready, k_taken = sem("k_ready"), sem("k_taken")
        vv_ready, vv_taken = sem("vv_ready"), sem("vv_taken")
        v_ready, v_gelu = sem("v_ready"), sem("v_gelu")
        u_ready, u_gelu = sem("u_ready"), sem("u_gelu")
        ssv_ready, stdv_ready, vn_ready = sem("ssv_ready"), sem("stdv_ready"), sem("vn_ready")
        z_ready, clip_ready, ln_ready, sp_ready = sem("z_ready"), sem("clip_ready"), sem("ln_ready"), sem("sp_ready")
        s_ready, low_ready, a_ready = sem("s_ready"), sem("low_ready"), sem("a_ready")
        av_ready, av_taken = sem("av_ready"), sem("av_taken")
        ws_turned, ws_ready = sem("ws_turned"), sem("ws_ready")
        gate_ready, gate_taken = sem("gate_ready"), sem("gate_taken")
        o_ready = sem("o_ready")
        pc_ready, pc_taken = sem("pc_ready"), sem("pc_taken")
        ph_ready, y_made = sem("ph_ready"), sem("y_made")
        pb_ready, zc_ready = sem("pb_ready"), sem("zc_ready")
        logits_ready, tops_ready, exps_ready = sem("logits_ready"), sem("tops_ready"), sem("exps_ready")
        chosen_ready, rank_ready, extra_ready = sem("chosen_ready"), sem("rank_ready"), sem("extra_ready")
        sel_ready, gathered, xg_ready = sem("sel_ready"), sem("gathered"), sem("xg_ready")
        wsel_ready, cmb_turned, cmb_ready = sem("wsel_ready"), sem("cmb_turned"), sem("cmb_ready")
        gu_ready, silu_ready, h_ready = sem("gu_ready"), sem("silu_ready"), sem("h_ready")
        h_turned, hhT_ready, y_ready, yy_ready = sem("h_turned"), sem("hhT_ready"), sem("y_ready"), sem("yy_ready")
        xs = [{n: sem(f"x{n}{l}") for n in (
            "landed", "gate", "sel", "gathered", "xg", "gu", "silu", "h", "turned", "evac", "y", "yy", "done")}
            for l in range(2)]

        block = ctx.enter_context(nc.Block())

        def slot(n):
            return ring[:, (n % RING) * SLOT:(n % RING + 1) * SLOT]

        def wide(n):
            return slot(n).rearrange("p (k f) -> p k f", k=K)

        def tall(n):
            return slot(n).rearrange("p (j d) -> p j d", j=4)

        def wait_landed(eng, n, turns=0):
            eng.wait_ge(landed[n % RING], (turns + (n // RING + 1)) * 16)

        @contextmanager
        def further(eng):
            total = eng.value_load(extra[0:1, 2 * NE:2 * NE + 1], min_val=0, max_val=MAX_TOTAL)

            @contextmanager
            def each():
                with eng.Fori(0, NE) as e:
                    blocks = eng.value_load(extra[0:1, bass.ds(e, 1)], min_val=0, max_val=MAX_MORE)
                    before = eng.value_load(extra[0:1, bass.ds(e + NE, 1)], min_val=0, max_val=MAX_TOTAL)
                    with eng.If(blocks > 0):
                        with eng.Fori(0, blocks) as r:
                            yield e, r, before + r + 1
                    eng.nop()

            each.total = total
            with eng.If(total > 0):
                yield each
            eng.nop()

        def after(l, e):
            return e + (NE * l + 1)

        def gates_used(l, e):
            return e + (TRI * TURNS * l + 1)

        def after_z(l, e):
            return e + ((NE + 1) * l + 2)

        def after_chunk(l, T, q):
            return T * CHUNKS + (CHUNKS * TRIS * l + q + 1)

        @block.sync
        def _(sp):
            def used_up(n):
                for l in range(2):
                    whole = L_MOE[l] + 3 * TRI * TURNS
                    if whole <= n < L_MOE[l] + PER_MOE:
                        e, mat = divmod(n - whole, 2)
                        return (gu_ready, y_ready)[mat], after(l, TURNS * TRI + e)
                    if L_MOE[l] <= n < whole:
                        e, mat = divmod(n - L_MOE[l], 3)
                        return ((gate_used, gates_used(l, e)), (gu_ready, after(l, e)), (y_ready, after(l, e)))[mat]
                if n < L_MOE[0]:
                    return ((q_ready, 2), (k_ready, 2), (vv_ready, 2), (v_ready, 2), (u_ready, 2),
                            (out_half, 1), (o_ready, TT))[n - L_EVEN]
                return ((pc_ready, 2), (ph_ready, 2), (pb_ready, 2), (pc_ready, 4), (ph_ready, 4), (pb_ready, 4),
                        (out_half, 2), (o_ready, 2 * TT + 1))[n - L_ODD]

            def load(n, src, dst):
                sp.dma_start(dst, src).then_inc(landed[n % RING], 16)

            def fill(n, src, dst):
                if n >= RING:
                    sp.wait_ge(*used_up(n - RING))
                load(n, src, dst)

            def cols(w, c):
                return w[:, c * 512:(c + 1) * 512].rearrange("(p k) f -> p k f", k=K)

            def outrows(w, r):
                return w[r * 512:(r + 1) * 512, :].rearrange("(j p) d -> p j d", p=P)

            def load_early(l, i):
                w = w_gate[l, TURNS * TRI + i].rearrange("(p k) f -> p k f", k=K)
                for half in range(2):
                    sp.dma_start(early[i][half].rearrange("p (k f) -> p k f", k=K // 2),
                                 w[:, K // 2 * half:K // 2 * (half + 1), :]).then_inc(early_landed[i], 16)

            def expert(l, b, i):
                e = b * TRI + i
                for mat, (w, used) in enumerate(((w_gate, gate_used), (w_up, gu_ready), (w_down, y_ready))):
                    n = L_MOE[l] + 3 * i + mat
                    src = w[l, e].rearrange("(j p) d -> p j d", p=P) if mat == 2 else \
                        w[l, e].rearrange("(p k) f -> p k f", k=K)
                    dst = tall(n) if mat == 2 else wide(n)
                    if isinstance(b, int):
                        if (i, mat) == (TRI - 1, 1):
                            sp.wait_ge(*((gate_taken, 4) if l == 0 else (pc_ready, 1)))
                            if l == 0:
                                sp.wait_ge(av_ready, 2)
                            load_early(l, 0)
                        fill(n, src, dst)
                    else:
                        sp.wait_ge(used, gates_used(l, e - TRI) if mat == 0 else after(l, e - TRI))
                        load(n, src, dst)

            def experts(l):
                for i in range(TRI):
                    expert(l, 0, i)
                sp.wait_ge(logits_ready, l + 1)
                load_early(l, 1)
                with sp.Fori(1, TURNS) as b:
                    for i in range(TRI):
                        expert(l, b, i)
                for i in range(REST):
                    n, e = L_MOE[l] + 3 * TRI * TURNS + 2 * i, TURNS * TRI + i
                    fill(n, w_up[l, e].rearrange("(p k) f -> p k f", k=K), wide(n))
                    fill(n + 1, w_down[l, e].rearrange("(j p) d -> p j d", p=P), tall(n + 1))
                X = xs[l]
                sp.wait_ge(extra_ready, l + 1)
                with further(sp) as each:
                    with each() as (e, r, n):
                        for mat, w in enumerate((w_gate, w_up, w_down)):
                            sp.wait_ge(X[("done", "gate", "gu")[mat]], n)
                            if mat < 2:
                                src = w[l, e].rearrange("(p k) f -> p k f", k=K)
                                dst = xb.rearrange("p (k f) -> p k f", k=K)
                            else:
                                src = w[l, e].rearrange("(j p) d -> p j d", p=P)
                                dst = xb.rearrange("p (j d) -> p j d", j=4)
                            sp.dma_start(dst, src).then_inc(X["landed"], 16)

            def small_loads():
                sp.dma_start(rows[0:24, :], odd_conv_w[0].rearrange("c (j p) -> (c j) p", p=P)).then_inc(smalls_loaded[2], 16)
                sp.dma_start(rows[24:28, :], gmlp_v_gain[0].rearrange("(j a) d -> j (a d)", a=2)).then_inc(smalls_loaded[3], 16)
                for l in range(2):
                    sp.dma_start(rgraw[:, l], router_group[l].rearrange("(p k) g -> p k g", k=K)).then_inc(smalls_loaded[5], 16)
                    sp.dma_start(reraw[:, l], router_expert[l].rearrange("g (p k) e -> p g k e", k=K)).then_inc(smalls_loaded[6], 16)

            for t in range(TT):
                sp.dma_start(x[:, t, :], x_in[0, t * P:(t + 1) * P, :]).then_inc(x_loaded[t], 16)
            sp.dma_start(gains[:, 0:4:2, :], norm_mix.rearrange("n (p k) -> p n k", k=K)).then_inc(smalls_loaded[0], 16)
            sp.dma_start(gains[:, 1:4:2, :], norm_ffn.rearrange("n (p k) -> p n k", k=K)).then_inc(smalls_loaded[1], 16)
            for n, c in enumerate((2, 3, 4, 1, 0)):
                fill(L_EVEN + n, cols(even_w_in[0], c), wide(L_EVEN + n))
                if n == 0:
                    small_loads()
            for r in range(2):
                fill(L_EVEN + 5 + r, outrows(even_w_out[0], r), tall(L_EVEN + 5 + r))
            experts(0)
            for n, c in enumerate((2, 4, 0, 3, 5, 1)):
                fill(L_ODD + n, cols(odd_w_in[0], c), wide(L_ODD + n))
            for r in range(2):
                fill(L_ODD + 6 + r, outrows(odd_w_out[0], r), tall(L_ODD + 6 + r))
            experts(1)
            fill(L_GAIN, norm_final.partition_broadcast(P), slot(L_GAIN)[:, 0:D])
            for t in range(TT):
                sp.wait_ge(final_ready, t + 1)
                sp.dma_start(out[0, t * P:(t + 1) * P, :], fin[:, t, :]).then_inc(out_stored, 16)
            sp.wait_ge(out_stored, 16 * TT)

        @block.gpsimd
        def _(pool):
            steps = [0]

            def link(ins):
                steps[0] += 1
                ins.then_inc(pool_step, 1)
                pool.wait_ge(pool_step, steps[0])

            def ramp(t, base, step, chan, op, fill):
                link(pool.affine_select(out=t[:, :], in_=t[:, :], compare_op=op, fill=fill, base=base,
                                        pattern=[[step, P]], channel_multiplier=chan))

            pool.memset(eps[:, :], EPS)
            pool.memset(ones[:, :], 1.0)
            pool.memset(nones[:, :], -1.0)
            pool.memset(nlin[:, :], -1.0)
            pool.memset(ident[:, :], 0.0)
            pool.memset(below[:, :], 1.0)
            pool.memset(upto[:, :], 1.0)
            pool.memset(diag[:, :], 0.0)
            link(pool.memset(cw[:, :], 0.0))
            ramp(ident, 0, -1, 1, ALU.not_equal, 1.0)
            ramp(below, 0, 1, -1, ALU.is_gt, 0.0)
            ramp(upto, 0, 1, -1, ALU.is_ge, 0.0)
            ramp(diag, 0, 1, -1, ALU.is_gt, -BIG)
            ramp(nlin, 0, -1, 1, ALU.is_ge, 0.0)
            pool.iota(count[:, :], [[1, S]], base=0, channel_multiplier=0, allow_small_or_imprecise_dtypes=True)
            pool.memset(pos[:, :], -1.0)
            link(pool.iota(rank32[:, :], [[-1, NE]], base=NE, channel_multiplier=0,
                           allow_small_or_imprecise_dtypes=True))
            pool.sem_inc(consts_ready, 1)
            for i in (5, 6):
                pool.wait_ge(smalls_loaded[i], 32)
            for l in range(2):
                pool.tensor_copy(rw[:, l, :, 0:G], rgraw[:, l])
                for g in range(G):
                    last = pool.tensor_copy(rw[:, l, :, G + EG * g:G + EG * (g + 1)], reraw[:, l, g])
            last.then_inc(router_ready, 1)

        @block.scalar
        def _(act):
            steps = [0]

            def link(ins):
                steps[0] += 1
                ins.then_inc(act_step, 1)
                act.wait_ge(act_step, steps[0])

            act.wait_ge(consts_ready, 1)

            preloads = [0]

            def preload(func):
                act.activation(junk[:, preloads[0]:preloads[0] + 1], eps[:, 0:1], func)
                preloads[0] += 1

            def roots(n):
                preload(ACT.Sqrt)
                for t in range(TT):
                    if n == 0:
                        act.wait_ge(x_loaded[t], 16)
                    else:
                        act.wait_ge(x_ready, TT * (n - 1) + t + 1)
                    link(act.activation(m[:, 0:D], x[:, t, :], ACT.Square, accum_out=ssq[:, t:t + 1]))
                    act.activation(ssq[:, t:t + 1], ssq[:, t:t + 1], ACT.Sqrt, bias=eps[:, 0:1],
                                   scale=1.0 / D).then_inc(std_ready, 1)

            def norm(n):
                roots(n)
                act.wait_ge(rstd_ready, TT * (n + 1))
                act.activation(hn[:, 1, HK:].rearrange("p k q -> p q k"),
                               x[:, 1, :].rearrange("p (q k) -> p q k", k=K)[:, :, HK:],
                               ACT.Copy, scale=rstd[:, 1:2]).then_inc(hn_act, 1)
                if n == 0:
                    act.wait_ge(smalls_loaded[0], 16)
                    act.wait_ge(smalls_loaded[1], 16)
                for j in (1, 3):
                    act.wait_ge(turned, 4 * n + j + 1)
                    for kk in range(2):
                        k = 2 * j + kk
                        last = act.activation(hT[:, k, :], bank[4 + j][:, kk * S:(kk + 1) * S], ACT.Copy,
                                              scale=gains[:, n, k:k + 1])
                    last.then_inc(hT_act, 1)
                preload((ACT.Exp, ACT.Exp, ACT.Silu, ACT.Exp)[n])

            def even():
                for j in range(2):
                    act.wait_ge(q_ready, j + 1)
                    act.activation(qT[:, 2 * j:2 * j + 2, :], bank[j][:, :].rearrange("p (j t) -> p j t", j=2),
                                   ACT.Copy, scale=HD ** -0.5).then_inc(q_taken, 1)

                def logs(h0):
                    for h in range(h0, h0 + 4):
                        act.wait_ge(clip_ready, h + 1)
                        ins = act.activation(att[h % 4], att[h % 4], ACT.Exp)
                        if h < h0 + 3:
                            link(ins)
                    link(ins)
                    for h in range(h0, h0 + 4):
                        act.activation(att[h % 4], att[h % 4], ACT.Ln, bias=1.0).then_inc(ln_ready, 1)

                def weights(h0):
                    for h in range(h0, h0 + 4):
                        blk = att[h % 4].rearrange("p (b t) -> p b t", b=3)
                        act.wait_ge(low_ready, h + 1)
                        act.activation(blk[:, 0:3:2, :], blk[:, 0:3:2, :], ACT.Exp)
                        act.activation(att[h % 4][:, P:2 * P], bank[h % 4][:, P:2 * P], ACT.Exp).then_inc(a_ready, 1)

                logs(0)
                weights(0)
                for t in range(TT):
                    act.wait_ge(v_ready, t + 1)
                    act.activation(v[:, t, :], bank[6 + t][:, :], ACT.Gelu).then_inc(v_gelu, 1)
                act.wait_ge(ssv_ready, 1)
                act.activation(ssv[:, :], ssv[:, :], ACT.Sqrt, bias=eps[:, 0:1], scale=1.0 / HD).then_inc(stdv_ready, 1)
                act.wait_ge(z_ready, NH)
                act.dma_start(ws, gmlp_w_s[0].rearrange("g t s -> t g s")).then_inc(ws_loaded, 16)
                for a in range(2):
                    src = gmlp_b_s[0].rearrange("(j a) t -> a j t", a=2)[a]
                    act.dma_start(bs[64 * a:64 * a + 64], src.partition_broadcast(HD)).then_inc(bs_loaded, 16)
                logs(4)
                for j in range(2):
                    act.wait_ge(u_ready, j + 1)
                    act.activation(uT[:, 2 * j:2 * j + 2, :], bank[4 + j][:, :].rearrange("p (j t) -> p j t", j=2),
                                   ACT.Gelu).then_inc(u_gelu, 1)
                weights(4)

            def odd():
                for s in range(2):
                    if s:
                        act.wait_ge(y_made, 2)
                    for j in range(2):
                        act.wait_ge(pc_ready, 2 * s + j + 1)
                        act.activation(cbuf[:, 2 * j:2 * j + 2, :], bank[j][:, :].rearrange("p (j t) -> p j t", j=2),
                                       ACT.Copy).then_inc(pc_taken, 1)

            def expert(l, e):
                act.wait_ge(gu_ready, after(l, e))
                act.activation(sg, GU[:, 0:FP], ACT.Silu).then_inc(silu_ready, 1)
                act.wait_ge(cmb_turned, after(l, e))
                act.activation(cmb, BB[:, 0:S], ACT.Copy).then_inc(cmb_ready, 1)
                act.wait_ge(h_turned, after(l, e))
                act.activation(hhT, BA[:, 0:P], ACT.Copy).then_inc(hhT_ready, 1)
                act.wait_ge(y_ready, after(l, e))
                act.activation(yy, YB[:, 0:DP], ACT.Copy).then_inc(yy_ready, 1)

            def moe(l):
                act.wait_ge(tops_ready, l + 1)
                for t in range(TT):
                    act.activation(gs[:, t, :], lg[:, t, 0:G], ACT.Exp, bias=gneg[:, t:t + 1], accum_out=gsum[:, t:t + 1])
                    last = act.activation(ex[:, t, :], ml[:, t, 0:NE], ACT.Exp, bias=eneg[:, t:t + 1])
                last.then_inc(exps_ready, 1)
                preload(ACT.Silu)
                with act.Fori(0, TURNS) as b:
                    for i in range(TRI):
                        expert(l, b * TRI + i)
                for i in range(REST):
                    expert(l, TURNS * TRI + i)
                X = xs[l]
                act.wait_ge(extra_ready, l + 1)
                with further(act) as each:
                    with each() as (e, r, n):
                        act.wait_ge(X["gu"], n)
                        act.activation(sg, GU[:, 0:FP], ACT.Silu).then_inc(X["silu"], 1)
                        act.wait_ge(X["turned"], n)
                        act.activation(cmb, BB[:, 0:S], ACT.Copy)
                        act.activation(hhT, BA[:, 0:P], ACT.Copy).then_inc(X["evac"], 1)
                        act.wait_ge(X["y"], n)
                        act.activation(yy, YB[:, 0:DP], ACT.Copy).then_inc(X["yy"], 1)
                    act.wait_ge(X["done"], each.total + 1)
                    preload(ACT.Sqrt)

            norm(0)
            even()
            norm(1)
            moe(0)
            norm(2)
            odd()
            norm(3)
            moe(1)
            preload(ACT.Sqrt)
            act.wait_ge(o_ready, 2 * (TT + 1))
            for t in range(TT):
                ins = act.activation(m[:, D * t:D * (t + 1)].rearrange("p (c d) -> p c d", c=NP), psum[:, 0:NP, DP * t:DP * (t + 1)],
                                     ACT.Square, accum_out=ssq[:, t:t + 1])
            link(ins)
            act.activation(ssq[:, :], ssq[:, :], ACT.Sqrt, bias=eps[:, 0:1], scale=1.0 / D).then_inc(std_ready, 1)

        @block.vector
        def _(dve):
            steps = [0]

            def link(ins):
                steps[0] += 1
                ins.then_inc(dve_step, 1)
                dve.wait_ge(dve_step, steps[0])

            def update(n, t):
                dve.wait_ge(o_ready, (TT + 1) * ((n - 1) // 2) + (t + 1 if n % 2 else TT + 1))
                src = psum[:, 2 * t:2 * t + 2, :] if n % 2 else psum[:, 0:NP, DP * t:DP * (t + 1)]
                xt = x[:, t, :].rearrange("p (c d) -> p c d", c=2 if n % 2 else NP)
                if n % 2:
                    dve.tensor_tensor(xt, src, xt, ALU.add).then_inc(x_ready, 1)
                else:
                    dve.tensor_copy(xt, src).then_inc(x_ready, 1)

            def norm(n):
                if n and n % 2 == 0:
                    for t in range(TT):
                        update(n, t)
                for t in range(TT):
                    if n % 2:
                        update(n, t)
                    dve.wait_ge(std_ready, TT * n + t + 1)
                    dve.reciprocal(rstd[:, t:t + 1], ssq[:, t:t + 1]).then_inc(rstd_ready, 1)
                    dve.wait_ge(rstd_ready, TT * n + t + 1)
                    ks = slice(0, K) if t == 0 else slice(0, HK)
                    dve.tensor_scalar(hn[:, t, ks].rearrange("p k q -> p q k"),
                                      x[:, t, :].rearrange("p (q k) -> p q k", k=K)[:, :, ks],
                                      rstd[:, t:t + 1], None, ALU.mult).then_inc(hn_dve, 1)
                if n == 0:
                    dve.wait_ge(smalls_loaded[0], 16)
                    dve.wait_ge(smalls_loaded[1], 16)
                for j in (0, 2):
                    dve.wait_ge(turned, 4 * n + j + 1)
                    dve.tensor_tensor(hT[:, 2 * j:2 * j + 2, :], bank[4 + j][:, :].rearrange("p (k t) -> p k t", k=2),
                                      gains[:, n, 2 * j:2 * j + 2].unsqueeze(2).to_broadcast([P, 2, S]),
                                      ALU.mult).then_inc(hT_dve, 1)

            def even():
                dve.wait_ge(cols_turned, 1)
                dve.tensor_copy(colsT[:, :], bank[0][:, 0:28]).then_inc(cols_ready, 1)
                for j in range(2):
                    dve.wait_ge(k_ready, j + 1)
                    dve.tensor_copy(kT[:, 2 * j:2 * j + 2, :],
                                    bank[6 + j][:, :].rearrange("p (j t) -> p j t", j=2)).then_inc(k_taken, 1)

                def clip(h0):
                    for h in range(h0, h0 + 4):
                        dve.wait_ge(z_ready, h + 1)
                        dve.tensor_scalar(att[h % 4], bank[h % 4][:, 0:384], LINEAR, None, ALU.min).then_inc(clip_ready, 1)

                def softplus(h0):
                    for h in range(h0, h0 + 4):
                        dve.wait_ge(ln_ready, h + 1)
                        link(dve.tensor_tensor(att[h % 4], bank[h % 4][:, 0:384], att[h % 4], ALU.max))
                        blk = att[h % 4].rearrange("p (b t) -> p b t", b=3)[:, 0:3:2, :]
                        dve.tensor_tensor(blk, blk, below[:, :].unsqueeze(1).to_broadcast([P, 2, P]),
                                          ALU.mult).then_inc(sp_ready, 1)

                def lows(h0):
                    for h in range(h0, h0 + 4):
                        dve.wait_ge(s_ready, h + 1)
                        dve.tensor_tensor(att[h % 4].rearrange("p (b t) -> p b t", b=3)[:, 0:3:2, :],
                                          bank[h % 4][:, 0:384].rearrange("p (b t) -> p b t", b=3)[:, 0:3:2, :],
                                          diag[:, :].unsqueeze(1).to_broadcast([P, 2, P]), ALU.min).then_inc(low_ready, 1)

                clip(0)
                softplus(0)
                for t in range(TT):
                    dve.wait_ge(vv_ready, t + 1)
                    dve.tensor_copy(vv[:, t, :], bank[4 + t][:, :]).then_inc(vv_taken, 1)
                lows(0)
                for t in range(TT):
                    dve.wait_ge(v_gelu, t + 1)
                    link(dve.tensor_tensor(vsq, v[:, t, :], v[:, t, :], ALU.mult))
                    ins = dve.tensor_reduce(ssv[:, NH * t:NH * (t + 1)], vsq.rearrange("p (g c) -> p g c", g=NH),
                                            AX_X, ALU.add)
                    ins.then_inc(ssv_ready, 1) if t == TT - 1 else link(ins)
                dve.wait_ge(stdv_ready, 1)
                link(dve.reciprocal(rsv[:, :], ssv[:, :]))
                for t in range(TT):
                    vg = v[:, t, :].rearrange("p (g c) -> p g c", g=NH)
                    dve.tensor_tensor(vg, vg, rsv[:, NH * t:NH * (t + 1)].unsqueeze(2).to_broadcast([P, NH, HD]),
                                      ALU.mult).then_inc(vn_ready, 1)
                dve.wait_ge(av_ready, 1)
                dve.tensor_copy(mixT[:, 4:6, :], bank[6][:, :].rearrange("p (j t) -> p j t", j=2)).then_inc(av_taken, 1)
                clip(4)
                softplus(4)
                dve.wait_ge(ws_turned, 1)
                for j in range(2):
                    dve.tensor_tensor(ws[:, 4 * j:4 * j + 4, :], bank[6 + j][:, :].rearrange("p (g t) -> p g t", g=4),
                                      upto[:, :].unsqueeze(1).to_broadcast([P, 4, P]), ALU.mult).then_inc(ws_ready, 1)
                lows(4)
                dve.wait_ge(bs_loaded, 32)
                dve.wait_ge(u_gelu, 2)
                dve.wait_ge(cols_ready, 1)
                for j in range(4):
                    if j % 2 == 0:
                        dve.wait_ge(gate_ready, j // 2 + 1)
                    g3 = bank[6 + j // 2][:, S * (j % 2):S * (j % 2 + 1)].rearrange("p (c t) -> p c t", c=2)
                    o3 = mixT[:, j, :].rearrange("p (c t) -> p c t", c=2)
                    link(dve.scalar_tensor_tensor(out=o3, in0=g3, scalar=colsT[:, 24 + j:25 + j],
                                                  in1=bs[:, j, :].unsqueeze(1).to_broadcast([P, 2, P]),
                                                  op0=ALU.mult, op1=ALU.add))
                    dve.tensor_tensor(mixT[:, j, :], mixT[:, j, :], uT[:, j, :], ALU.mult).then_inc(gate_taken, 1)
                dve.wait_ge(av_ready, 2)
                dve.tensor_copy(mixT[:, 6:8, :], bank[4][:, :].rearrange("p (j t) -> p j t", j=2)).then_inc(av_taken, 1)

            def odd():
                link(dve.memset(ybuf[:, :, 0:PAD], 0.0))
                for s in range(2):
                    for j in range(2):
                        dve.wait_ge(ph_ready, 2 * s + j + 1)
                        dve.wait_ge(pc_taken, 2 * s + j + 1)
                        dve.tensor_tensor(ybuf[:, 2 * j:2 * j + 2, PAD:], bank[2 + j][:, :].rearrange("p (j t) -> p j t", j=2),
                                          cbuf[:, 2 * j:2 * j + 2, :], ALU.mult).then_inc(y_made, 1)
                    dve.wait_ge(y_made, 2 * s + 2)
                    for tap in range(CONV):
                        for j in range(4):
                            w = colsT[:, tap * K + 4 * s + j:tap * K + 4 * s + j + 1]
                            src = ybuf[:, j, tap:tap + S]
                            if tap == 0:
                                ins = dve.tensor_scalar(cv[:, j, :], src, w, None, ALU.mult)
                            else:
                                ins = dve.scalar_tensor_tensor(out=cv[:, j, :], in0=src, scalar=w, in1=cv[:, j, :],
                                                               op0=ALU.mult, op1=ALU.add)
                        link(ins)
                    for j in range(2):
                        dve.wait_ge(pb_ready, 2 * s + j + 1)
                        dve.tensor_tensor(mixT[:, 4 * s + 2 * j:4 * s + 2 * j + 2, :],
                                          bank[4 + j][:, :].rearrange("p (j t) -> p j t", j=2),
                                          cv[:, 2 * j:2 * j + 2, :], ALU.mult).then_inc(zc_ready, 1)

            def fillers():
                for lt in (ml[:, :, NE:], pair8[:, :, 2:]):
                    ins = dve.memset(lt, -4 * BIG)
                link(ins)

            def route(l):
                dve.wait_ge(logits_ready, l + 1)
                link(dve.tensor_copy(lg, bank[4][:, 0:TT * (G + NE)].rearrange("p (t e) -> p t e", t=TT)))
                link(dve.tensor_reduce(gmax, lg[:, :, 0:G], AX_X, ALU.max))
                for t in range(TT):
                    ins = dve.scalar_tensor_tensor(out=gs[:, t, :], in0=lg[:, t, 0:G], scalar=gmax[:, t:t + 1],
                                                   in1=rank32[:, 0:G], op0=ALU.is_equal, op1=ALU.mult)
                link(ins)
                link(dve.tensor_reduce(gidx, gs, AX_X, ALU.max))
                for t in range(TT):
                    ins = dve.tensor_scalar(pen[:, t, :], rank32[:, 0:G], gidx[:, t:t + 1], -BIG,
                                            ALU.not_equal, ALU.mult)
                link(ins)
                for t in range(TT):
                    ins = dve.tensor_tensor(ml[:, t, 0:NE].rearrange("p (g e) -> p g e", g=G),
                                            lg[:, t, G:].rearrange("p (g e) -> p g e", g=G),
                                            pen[:, t, :].unsqueeze(2).to_broadcast([P, G, EG]), ALU.add)
                link(ins)
                for t in range(TT):
                    ins = dve.max(top8[:, t, :], ml[:, t, :])
                link(ins)
                link(dve.tensor_copy(pair8[:, :, 0:2], top8[:, :, 0:2]))
                for t in range(TT):
                    ins = dve.match_replace(mr[:, t, :], pair8[:, t, :], ml[:, t, :], -8 * BIG)
                link(ins)
                dve.tensor_scalar(chosen, mr[:, :, 0:NE], -6 * BIG, None, ALU.is_lt).then_inc(chosen_ready, 1)
                dve.tensor_scalar(gneg, gmax, -1.0, None, ALU.mult)
                dve.tensor_scalar(eneg, top8[:, :, 0:1].rearrange("p t o -> p (t o)"), -1.0, None,
                                  ALU.mult).then_inc(tops_ready, 1)
                pos3 = pos[:, :].rearrange("p (t e) -> p t e", t=TT)[:, :, 0:NE]
                dve.wait_ge(rank_ready, l + 1)
                link(dve.scalar_tensor_tensor(out=rk, in0=bank[5][:, 0:TT * NE].rearrange("p (t e) -> p t e", t=TT),
                                              scalar=1.0, in1=chosen, op0=ALU.add, op1=ALU.mult))
                link(dve.tensor_scalar(pos3, rk, -1.0, None, ALU.add))

            def expert_weights(l):
                dve.wait_ge(exps_ready, l + 1)
                link(dve.tensor_tensor(ex, ex, chosen, ALU.mult))
                link(dve.tensor_reduce(den, ex, AX_X, ALU.add))
                link(dve.tensor_tensor(den, den, gsum, ALU.mult))
                link(dve.reciprocal(den, den))
                link(dve.tensor_tensor(cw[:, :].rearrange("p (t e) -> p t e", t=TT)[:, :, 0:NE], ex,
                                       den.unsqueeze(2).to_broadcast([P, TT, NE]), ALU.mult))

            def more_blocks(l):
                limits = count[:, CAP:CAP * MAX_MORE + 1:CAP]
                counts = bank[5][:, TT * NE:TT * NE + NE]
                link(dve.tensor_tensor(over, counts.unsqueeze(2).to_broadcast([P, NE, MAX_MORE]),
                                       limits.unsqueeze(1).to_broadcast([P, NE, MAX_MORE]), ALU.is_gt))
                link(dve.tensor_reduce(more, over, AX_X, ALU.add))
                for buf in sums:
                    link(dve.memset(buf, 0.0))
                link(dve.tensor_copy(sums[0][:, HALO:], more))
                step, n = 1, 0
                while step < NE:
                    src, dst = sums[n % 2], sums[(n + 1) % 2]
                    link(dve.tensor_tensor(dst[:, HALO:], src[:, HALO:], src[:, HALO - step:HALO - step + NE], ALU.add))
                    step, n = 2 * step, n + 1
                total = sums[n % 2]
                link(dve.tensor_copy(extra[:, 0:NE], more))
                link(dve.tensor_tensor(extra[:, NE:2 * NE], total[:, HALO:], more, ALU.subtract))
                link(dve.tensor_copy(extra[:, 2 * NE:], total[:, HALO + NE - 1:]))
                dve.sem_inc(extra_ready, 1)

            def at(e, t):
                return (e + t * (NE + 1))

            def select(l, T):
                for i in range(TRI):
                    for t in range(TT):
                        c = at(T * TRI + i, t)
                        last = dve.tensor_scalar(sel[:, t, CAP * i:CAP * (i + 1)], count[:, 0:CAP],
                                                 pos[:, bass.ds(c, 1)], None, ALU.is_equal)
                last.then_inc(sel_ready, 1)

            def weigh(l, e):
                for t in range(TT):
                    c = at(e, t)
                    last = dve.tensor_scalar(wsel[:, t, :].rearrange("p (n c) -> p n c", n=NP),
                                             count[:, 0:CAP].unsqueeze(1).to_broadcast([P, NP, CAP]),
                                             pos[:, bass.ds(c, 1)], cw[:, bass.ds(c, 1)], ALU.is_equal, ALU.mult)
                last.then_inc(wsel_ready, 1)

            def gather(l, T):
                for q in range(CHUNKS):
                    dve.wait_ge(gathered, after_chunk(l, T, q))
                    b = (BA, BB)[q % 2]
                    dve.tensor_tensor(xg[:, KC * q:KC * (q + 1), :],
                                      b[:, 0:KC * TRI * CAP].rearrange("p (k c) -> p k c", k=KC),
                                      gains[:, 2 * l + 1, KC * q:KC * (q + 1)].unsqueeze(2).to_broadcast([P, KC, TRI * CAP]),
                                      ALU.mult).then_inc(xg_ready, 1)

            def expert(l, T, i, last_turn=False, last=False):
                e = T * TRI + i
                if i == 0 and not last_turn:
                    select(l, T + 1)
                dve.wait_ge(gu_ready, after(l, e))
                dve.wait_ge(silu_ready, after(l, e))
                dve.tensor_tensor(hh, GU[:, FP:2 * FP], sg, ALU.mult).then_inc(h_ready, 1)
                if i == TRI - 1:
                    gather(l, T + 1)
                if not last:
                    dve.wait_ge(cmb_turned, after(l, e))
                    weigh(l, e + 1)

            def moe(l):
                dve.memset(cmb, 0.0).then_inc(cmb_ready, 1)
                dve.memset(yy, 0.0).then_inc(yy_ready, 1)
                fillers()
                route(l)
                select(l, 0)
                expert_weights(l)
                weigh(l, 0)
                gather(l, 0)
                more_blocks(l)
                with dve.Fori(0, TURNS) as b:
                    for i in range(TRI):
                        expert(l, b, i)
                for i in range(REST):
                    expert(l, TURNS, i, last_turn=True, last=i == REST - 1)
                X = xs[l]
                with further(dve) as each:
                    with each() as (e, r, n):
                        dve.wait_ge(X["done"], n)
                        for t in range(TT):
                            c = at(e, t)
                            ranks = count[:, bass.ds((r + 1) * CAP, CAP)]
                            dve.tensor_scalar(sel[:, t, 0:CAP], ranks, pos[:, bass.ds(c, 1)], None, ALU.is_equal)
                            last = dve.tensor_scalar(wsel[:, t, :].rearrange("p (n c) -> p n c", n=NP),
                                                     ranks.unsqueeze(1).to_broadcast([P, NP, CAP]),
                                                     pos[:, bass.ds(c, 1)], cw[:, bass.ds(c, 1)], ALU.is_equal, ALU.mult)
                        last.then_inc(X["sel"], 1)
                        dve.wait_ge(X["gathered"], n)
                        dve.tensor_tensor(xg[:, :, 0:CAP], BA[:, 0:K * CAP].rearrange("p (k c) -> p k c", k=K),
                                          gains[:, 2 * l + 1, :].unsqueeze(2).to_broadcast([P, K, CAP]),
                                          ALU.mult).then_inc(X["xg"], 1)
                        dve.wait_ge(X["gu"], n)
                        dve.wait_ge(X["silu"], n)
                        dve.tensor_tensor(hh, GU[:, FP:2 * FP], sg, ALU.mult).then_inc(X["h"], 1)
                    dve.wait_ge(X["done"], each.total + 1)
                    dve.tensor_copy(more[:, 0:1], more[:, 0:1])

            dve.wait_ge(consts_ready, 1)
            for t in range(TT):
                dve.wait_ge(x_loaded[t], 16)
            norm(0)
            even()
            norm(1)
            moe(0)
            norm(2)
            odd()
            norm(3)
            moe(1)
            dve.wait_ge(std_ready, 4 * TT + 1)
            link(dve.reciprocal(rstd[:, :], ssq[:, :]))
            wait_landed(dve, L_GAIN)
            for t in range(TT):
                dve.scalar_tensor_tensor(out=fin[:, t, :].rearrange("p (c d) -> p c d", c=NP),
                                         in0=psum[:, 0:NP, DP * t:DP * (t + 1)], scalar=rstd[:, t:t + 1],
                                         in1=slot(L_GAIN)[:, 0:D].rearrange("p (c d) -> p c d", c=NP),
                                         op0=ALU.mult, op1=ALU.mult).then_inc(final_ready, 1)

        @block.tensor
        def _(pe):
            def norm(n):
                def turn(t):
                    for j in range(4):
                        for kk in range(2):
                            last = pe.transpose(bank[4 + j][:, kk * S + t * P:kk * S + (t + 1) * P],
                                                hn[:, t, 2 * j + kk, :], ident[:, :])
                        if t:
                            last.then_inc(turned, 1)

                pe.wait_ge(hn_dve, TT * n + 1)
                turn(0)
                if n % 2:
                    pe.wait_ge(x_ready, TT * n)
                    for t in range(TT):
                        for part in range(NP):
                            pe.matmul(bank[part][:, DP * t:DP * (t + 1)], ident[:, :], x[:, t, DP * part:DP * (part + 1)],
                                      start=t == 0, stop=False, skip_group_check=True)
                pe.wait_ge(hn_dve, TT * n + 2)
                pe.wait_ge(hn_act, n + 1)
                turn(1)

            def wait_hT(n, k):
                if k % 2 == 0:
                    pe.wait_ge((hT_dve, hT_act)[k // 2 % 2], 2 * n + k // 4 + 1)

            def channels(n, banks, ready, norms=None):
                wait_landed(pe, n)
                for c in range(4):
                    for k in range(K):
                        if c == 0 and norms is not None:
                            wait_hT(norms, k)
                        last = pe.matmul(bank[banks[c // 2]][:, (c % 2) * S:(c % 2 + 1) * S],
                                         wide(n)[:, k, P * c:P * (c + 1)], hT[:, k, :], start=k == 0, stop=k == K - 1)
                    if c % 2:
                        last.then_inc(ready, 1)

            def tokens(n, banks, ready):
                wait_landed(pe, n)
                for t in range(TT):
                    for k in range(K):
                        last = pe.matmul(bank[banks[t]][:, :], hT[:, k, P * t:P * (t + 1)], wide(n)[:, k, :],
                                         start=k == 0, stop=k == K - 1)
                    last.then_inc(ready, 1)

            def project_out(n, second_half):
                for r in range(2):
                    wait_landed(pe, n + r)
                    if r == 1:
                        second_half()
                    order = [(j, t) for j in range(4) for t in range(TT)] if r == 0 else \
                        [(j, t) for t in range(TT) for j in range(4)]
                    for j, t in order:
                        for c in range(2):
                            last = pe.matmul(bank[2 * t + c][:, :], mixT[:, 4 * r + j, P * t:P * (t + 1)],
                                             tall(n + r)[:, j, 512 * c:512 * (c + 1)],
                                             start=r == 0 and j == 0, stop=r == 1 and j == 3)
                        if r == 1 and j == 3:
                            last.then_inc(o_ready, 1)
                    if r == 0:
                        last.then_inc(out_half, 1)

            def even():
                L = L_EVEN
                channels(L, (0, 1), q_ready, norms=0)
                channels(L + 1, (6, 7), k_ready)

                def scores(h0):
                    for h in range(h0, h0 + 4, 2):
                        for keys in range(2):
                            for one in (h, h + 1):
                                r, c = slice(HD * (one % 2), HD * (one % 2 + 1)), one // 2
                                b = bank[one % 4]
                                lo = P * keys
                                last = pe.matmul(b[:, S * keys:S * keys + S - lo], kT[r, c, lo:lo + P], qT[r, c, lo:S],
                                                 start=keys == 0, stop=False, skip_group_check=True)
                                if keys:
                                    last.then_inc(z_ready, 1)

                def suffixes(h):
                    a, b = att[h % 4], bank[h % 4]
                    pe.wait_ge(sp_ready, h + 1)
                    pe.matmul(b[:, 0:S], nlin[:, :], a[:, 0:S], start=False, stop=False, skip_group_check=True)
                    pe.matmul(b[:, P:S], nones[:, :], a[:, S:S + P], start=False, stop=False, skip_group_check=True)
                    pe.matmul(b[:, S:S + P], nlin[:, :], a[:, S:S + P], start=False, stop=True,
                              skip_group_check=True).then_inc(s_ready, 1)

                def values(h0, b):
                    for h in range(h0, h0 + 4, 2):
                        pe.wait_ge(a_ready, h + 2)
                        for keys in range(2):
                            for one in (h, h + 1):
                                lo = P * keys
                                o = bank[b][HD * (one % 2):HD * (one % 2 + 1), S * (h % 4 // 2):S * (h % 4 // 2 + 1)]
                                last = pe.matmul(o[:, lo:S], vv[:, keys, HD * one:HD * (one + 1)],
                                                 att[one % 4][:, S * keys:S * keys + S - lo], start=keys == 0,
                                                 stop=keys == 1, skip_group_check=True)
                    last.then_inc(av_ready, 1)

                pe.wait_ge(q_taken, 2)
                pe.wait_ge(k_taken, 2)
                scores(0)
                tokens(L + 2, (4, 5), vv_ready)
                for h in range(4):
                    suffixes(h)
                tokens(L + 3, (6, 7), v_ready)
                pe.wait_ge(vv_taken, 2)
                pe.wait_ge(v_gelu, 1)
                values(0, 6)
                scores(4)
                channels(L + 4, (4, 5), u_ready)
                pe.wait_ge(ws_loaded, 16)
                pe.wait_ge(av_taken, 1)
                pe.wait_ge(v_gelu, 2)
                for g in range(NH):
                    last = pe.transpose(bank[6 + g // 4][:, P * (g % 4):P * (g % 4 + 1)], ws[:, g, :], ident[:, :])
                last.then_inc(ws_turned, 1)
                for h in range(4, 8):
                    suffixes(h)
                pe.wait_ge(ws_ready, 2)
                pe.wait_ge(vn_ready, 2)
                for j in range(4):
                    for c in range(2):
                        for g in (2 * j, 2 * j + 1):
                            last = pe.matmul(bank[6 + j // 2][HD * (g % 2):HD * (g % 2 + 1),
                                                              S * (j % 2) + P * c:S * (j % 2) + P * (c + 1)],
                                             v[:, c, HD * g:HD * (g + 1)], ws[:, g, :], start=True, stop=True)
                    if j % 2:
                        last.then_inc(gate_ready, 1)
                pe.wait_ge(u_gelu, 1)
                values(4, 4)
                pe.wait_ge(gate_taken, 4)
                project_out(L + 5, lambda: pe.wait_ge(av_taken, 2))

            def odd():
                L = L_ODD
                for s in range(2):
                    if s:
                        pe.wait_ge(pc_taken, 2)
                    channels(L + 3 * s, (0, 1), pc_ready, norms=None if s else 2)
                    if s:
                        pe.wait_ge(y_made, 2)
                    channels(L + 3 * s + 1, (2, 3), ph_ready)
                    if s:
                        pe.wait_ge(zc_ready, 2)
                    channels(L + 3 * s + 2, (4, 5), pb_ready)
                pe.wait_ge(y_made, 4)
                pe.wait_ge(zc_ready, 2)
                project_out(L + 6, lambda: pe.wait_ge(zc_ready, 4))

            def gate_up(w_of, block_of, lo):
                for k in range(K):
                    for part in range(NP):
                        last = pe.matmul(GU[CAP * part:CAP * (part + 1), lo:lo + FP], block_of(k),
                                         w_of(k)[:, FP * part:FP * (part + 1)], start=k == 0, stop=k == K - 1)
                return last

            def down(w):
                for f in range(NP):
                    for part in range(NP):
                        last = pe.matmul(YB[CAP * part:CAP * (part + 1), 0:DP], hhT[:, CAP * f:CAP * (f + 1)],
                                         w[:, f, DP * part:DP * (part + 1)], start=f == 0, stop=f == NP - 1)
                return last

            def scatter():
                for t in range(TT):
                    for part in range(NP):
                        r = slice(CAP * part, CAP * (part + 1))
                        last = pe.matmul(bank[part][:, DP * t:DP * (t + 1)], cmb[r, P * t:P * (t + 1)], yy[r, :],
                                         start=False, stop=False, skip_group_check=True)
                return last

            def turn_wsel():
                for t in range(TT):
                    last = pe.transpose(BB[:, P * t:P * (t + 1)], wsel[:, t, :], ident[:, :])
                return last

            def turn_h():
                return pe.transpose(BA[:, 0:P], hh, ident[:, :])

            def gather(l, T):
                pe.wait_ge(sel_ready, T + (TRIS * l + 1))
                for q in range(CHUNKS):
                    if q >= 2:
                        pe.wait_ge(xg_ready, after_chunk(l, T, q - 2))
                    b = (BA, BB)[q % 2]
                    for kk in range(KC):
                        for t in range(TT):
                            last = pe.matmul(b[:, kk * TRI * CAP:(kk + 1) * TRI * CAP], hn[:, t, KC * q + kk, :],
                                             sel[:, t, :], start=t == 0, stop=t == TT - 1)
                    last.then_inc(gathered, 1)

            def expert(l, T, i, rest=False):
                e = T * TRI + i
                n, turns = (L_MOE[l] + 3 * TRI * TURNS + 2 * i - 1, 0) if rest else (L_MOE[l] + 3 * i, T)
                block_of = lambda k: xg[:, k, CAP * i:CAP * (i + 1)]
                if rest:
                    pe.wait_ge(early_landed[i], 32 * (l + 1))
                    halves = [w.rearrange("p (k f) -> p k f", k=K // 2) for w in early[i]]
                    gate_up(lambda k: halves[k // (K // 2)][:, k % (K // 2), :], block_of, 0)
                else:
                    wait_landed(pe, n, turns)
                    gate_up(lambda k: wide(n)[:, k, :], block_of, 0).then_inc(gate_used, 1)
                wait_landed(pe, n + 1, turns)
                gate_up(lambda k: wide(n + 1)[:, k, :], block_of, FP).then_inc(gu_ready, 1)
                pe.wait_ge(yy_ready, after_z(l, e - 1))
                pe.wait_ge(cmb_ready, after_z(l, e - 1))
                scatter()
                pe.wait_ge(wsel_ready, after(l, e))
                turn_wsel().then_inc(cmb_turned, 1)
                if i == TRI - 1:
                    pe.wait_ge(cmb_ready, after_z(l, e))
                    gather(l, T + 1)
                    pe.wait_ge(xg_ready, after_chunk(l, T + 1, 0))
                pe.wait_ge(h_ready, after(l, e))
                turn_h().then_inc(h_turned, 1)
                pe.wait_ge(hhT_ready, after(l, e))
                wait_landed(pe, n + 2, turns)
                down(tall(n + 2)).then_inc(y_ready, 1)
                if i == TRI - 1:
                    pe.wait_ge(xg_ready, after_chunk(l, T + 1, CHUNKS - 1))

            def moe(l):
                pe.wait_ge(router_ready, 1)
                for t in range(TT):
                    for k in range(K):
                        if t == 0:
                            wait_hT(2 * l + 1, k)
                        last = pe.matmul(bank[4][:, (G + NE) * t:(G + NE) * (t + 1)], hT[:, k, P * t:P * (t + 1)],
                                         rw[:, l, k, :], start=k == 0, stop=k == K - 1)
                last.then_inc(logits_ready, 1)
                pe.wait_ge(chosen_ready, l + 1)
                b = bank[5]
                pe.matmul(b[:, 0:NE], below[:, :], chosen[:, 0, :], start=True, stop=True)
                pe.matmul(b[:, NE:2 * NE], ones[:, :], chosen[:, 0, :], start=True, stop=False)
                pe.matmul(b[:, NE:2 * NE], below[:, :], chosen[:, 1, :], start=False, stop=True)
                for t in range(TT):
                    last = pe.matmul(b[:, 2 * NE:3 * NE], ones[:, :], chosen[:, t, :], start=t == 0, stop=t == TT - 1)
                last.then_inc(rank_ready, 1)
                gather(l, 0)
                pe.wait_ge(xg_ready, after_chunk(l, 0, CHUNKS - 1))
                with pe.Fori(0, TURNS) as T:
                    for i in range(TRI):
                        expert(l, T, i)
                for i in range(REST):
                    expert(l, TURNS, i, rest=True)
                pe.wait_ge(yy_ready, after_z(l, NE - 1))
                pe.wait_ge(cmb_ready, after_z(l, NE - 1))
                X = xs[l]
                scatter().then_inc(o_ready, 1)
                pe.wait_ge(extra_ready, l + 1)
                with further(pe) as each:
                    xw, xt = xb.rearrange("p (k f) -> p k f", k=K), xb.rearrange("p (j d) -> p j d", j=4)
                    pe.sem_inc(X["done"], 1)
                    with each() as (e, r, n):
                        pe.wait_ge(X["sel"], n)
                        for k in range(K):
                            for t in range(TT):
                                last = pe.matmul(BA[:, CAP * k:CAP * (k + 1)], hn[:, t, k, :], sel[:, t, 0:CAP],
                                                 start=t == 0, stop=t == TT - 1)
                        last.then_inc(X["gathered"], 1)
                        pe.wait_ge(X["xg"], n)
                        for mat in range(2):
                            pe.wait_ge(X["landed"], n * 48 - 16 * (2 - mat))
                            gate_up(lambda k: xw[:, k, :], lambda k: xg[:, k, 0:CAP], FP * mat).then_inc(X[("gate", "gu")[mat]], 1)
                        turn_wsel()
                        pe.wait_ge(X["h"], n)
                        turn_h().then_inc(X["turned"], 1)
                        pe.wait_ge(X["evac"], n)
                        pe.wait_ge(X["landed"], n * 48)
                        down(xt).then_inc(X["y"], 1)
                        pe.wait_ge(X["yy"], n)
                        scatter().then_inc(X["done"], 1)

            pe.wait_ge(consts_ready, 1)
            pe.wait_ge(smalls_loaded[2], 16)
            pe.wait_ge(smalls_loaded[3], 16)
            pe.transpose(bank[0][:, 0:28], rows[:, :], ident[0:28, 0:28]).then_inc(cols_turned, 1)
            norm(0)
            pe.wait_ge(cols_ready, 1)
            even()
            norm(1)
            moe(0)
            norm(2)
            odd()
            norm(3)
            moe(1)


NAMES = ("x", "even_w_in", "even_w_out", "gmlp_w_s", "gmlp_b_s", "gmlp_v_gain", "odd_w_in", "odd_conv_w",
         "odd_w_out", "norm_mix", "norm_ffn", "router_group", "router_expert", "w_gate", "w_up", "w_down",
         "norm_final")


def kernel(**inputs):
    import numpy as np
    import concourse.bacc as bacc
    from concourse.bass_utils import run_bass_kernel_spmd

    nc = bacc.Bacc("TRN2", target_bir_lowering=False, num_devices=1)
    arrays, args = {}, []
    for name in NAMES:
        a = np.ascontiguousarray(inputs[name])
        arrays[f"in_{name}"] = a
        args.append(nc.dram_tensor(f"in_{name}", a.shape, mybir.dt.from_np(a.dtype), kind="ExternalInput").ap())
    args.append(nc.dram_tensor("out", (1, S, D), F32, kind="ExternalOutput").ap())
    trunk(nc, *args)
    return run_bass_kernel_spmd(nc, [arrays], core_ids=[0]).results[0]["out"]
```

```python
from contextlib import ExitStack, contextmanager

import concourse.bass as bass
from concourse import mybir

F32 = mybir.dt.float32
F32R = mybir.dt.float32r
I32 = mybir.dt.int32
ALU = mybir.AluOpType
ACT = mybir.ActivationFunctionType
AX_X = mybir.AxisListType.X

P = 128
D = 1024
S = 256
TT = S // P
K = D // P
HK = K // 2
HD = 64
NH = 8
G = 4
EG = 8
NE = G * EG
FF = 512
CAP = 32
NP = P // CAP
FP = FF // NP
DP = D // NP
CONV = 3
EPS = 1e-6
BIG = 1e30
LINEAR = 40.0
RING = 9
LAG = 2
SLOT = 4096
TRI = 3
TRIS = -(-NE // TRI)
TURNS = TRIS - 2
CHUNKS = 2
KC = K // CHUNKS
MAX_MORE = (S - 1) // CAP
MAX_TOTAL = 2 * S // CAP

L_EVEN = 0
EARLY = TURNS * TRI
PER_MOE = 3 * NE - 2
L_MOE = [7, 7 + PER_MOE + 8]
L_ODD = 7 + PER_MOE
L_GAIN = L_MOE[1] + PER_MOE


def trunk(nc, x_in, even_w_in, even_w_out, gmlp_w_s, gmlp_b_s, gmlp_v_gain, odd_w_in, odd_conv_w,
          odd_w_out, norm_mix, norm_ffn, router_group, router_expert, w_gate, w_up, w_down,
          norm_final, out):
    with ExitStack() as ctx:
        def sb(name, cols, dt=F32, rows=P):
            return ctx.enter_context(nc.sbuf_tensor(name, [rows, cols], dt))

        def sem(name):
            return ctx.enter_context(nc.semaphore(name))

        def sb_halves(name, cols, pieces=1):
            with ExitStack() as first:
                halves = [first.enter_context(nc.sbuf_tensor(f"{name}_halves{i}", [P, cols // pieces], F32R))
                          for i in range(pieces)]
            return sb(name, cols), *halves

        ring, *slot_halves = sb_halves("ring", RING * SLOT, RING)
        x_flat = sb("x", TT * D)
        x = x_flat[:, :].rearrange("p (t d) -> p t d", t=TT)
        hn_flat, hn_halves = sb_halves("hn", TT * D)
        hn = hn_flat[:, :].rearrange("p (t k q) -> p t k q", t=TT, k=K)
        fin = hn_flat[:, :].rearrange("p (t d) -> p t d", t=TT)
        scr, scr_halves = sb_halves("scr", 4096)
        hT = scr[:, 0:2048].rearrange("p (k t) -> p k t", k=K)
        att = [scr[:, 2048 + 384 * i:2048 + 384 * (i + 1)] for i in range(4)]
        vsq = scr[:, 3584:4096]
        xb = scr[:, :]
        m, m_halves = sb_halves("m", 5128)
        early = ((scr[:, 2048:4096], m[:, 3080:5128]),
                 (scr[:, 0:2048], x_flat[:, :]))
        hT_hi = scr_halves[:, 0:2048].rearrange("p (k t) -> p k t", k=K)
        hT_lo = [w.rearrange("p (k t) -> p k t", k=K) for w in (hn_halves[:, :], scr_halves[:, 2048:4096])]
        mix_hi = [w.rearrange("p (j t) -> p j t", j=K) for w in (scr_halves[:, 0:2048], hn_halves[:, :])]
        mix_lo = [w.rearrange("p (j t) -> p j t", j=K) for w in (hn_halves[:, :], m_halves[:, 3080:5128])]
        uT = m[:, 0:1024].rearrange("p (j t) -> p j t", j=4)
        v = m[:, 1024:2048].rearrange("p (t c) -> p t c", t=TT)
        qT = m[:, 2048:3072].rearrange("p (j t) -> p j t", j=4)
        kT = m[:, 3072:4096].rearrange("p (j t) -> p j t", j=4)
        vv = m[:, 4096:5120].rearrange("p (t c) -> p t c", t=TT)
        ws = m[:, 2048:3072].rearrange("p (g s) -> p g s", g=NH)
        bs = m[:, 3072:3584].rearrange("p (j t) -> p j t", j=4)
        cbuf = m[:, 0:1024].rearrange("p (j t) -> p j t", j=4)
        PAD = CONV - 1
        ybuf = m[:, 1024:1024 + 4 * (S + PAD)].rearrange("p (j t) -> p j t", j=4)
        cv = m[:, 2056:3080].rearrange("p (j t) -> p j t", j=4)
        used_m = [0]

        def temp(cols):
            at = used_m[0]
            used_m[0] += cols
            assert used_m[0] <= 3080
            return m[:, at:at + cols]

        xg = temp(K * TRI * CAP).rearrange("p (k c) -> p k c", k=K)
        sel = temp(TT * TRI * CAP).rearrange("p (t c) -> p t c", t=TT)
        wsel = temp(TT * P).rearrange("p (t c) -> p t c", t=TT)
        cmb = temp(TT * P)
        sg = temp(FP)
        hh = temp(FP)
        hhT = temp(P)
        yy = temp(DP)
        lg = temp(TT * (G + NE)).rearrange("p (t e) -> p t e", t=TT)
        TAIL = 6
        ml = temp(TT * (NE + TAIL)).rearrange("p (t e) -> p t e", t=TT)
        mr = temp(TT * (NE + TAIL)).rearrange("p (t e) -> p t e", t=TT)
        top8 = temp(TT * 8).rearrange("p (t e) -> p t e", t=TT)
        pair8 = temp(TT * 8).rearrange("p (t e) -> p t e", t=TT)
        chosen = temp(TT * NE).rearrange("p (t e) -> p t e", t=TT)
        ex = temp(TT * NE).rearrange("p (t e) -> p t e", t=TT)
        rk = temp(TT * NE).rearrange("p (t e) -> p t e", t=TT)
        gs = temp(TT * G).rearrange("p (t g) -> p t g", t=TT)
        pen = temp(TT * G).rearrange("p (t g) -> p t g", t=TT)
        (gmax, gneg, gidx, eneg, gsum, den) = (temp(TT) for _ in range(6))
        over = temp(NE * MAX_MORE).rearrange("p (e r) -> p e r", e=NE)
        more = temp(NE)
        HALO = NE // 2
        sums = [temp(HALO + NE) for _ in range(2)]

        ident, below, upto, nlin, ones, nones, diag = (sb(n, P) for n in (
            "ident", "below", "upto", "nlin", "ones", "nones", "diag"))
        count = sb("count", S)
        rank32 = sb("rank32", NE)
        eps = sb("eps", 1)
        gains = sb("gains", 4 * K)[:, :].rearrange("p (n k) -> p n k", n=4)
        rows = sb("rows", P, rows=28)
        colsT = sb("colsT", 28)
        rgraw = sb("rgraw", 2 * K * G)[:, :].rearrange("p (l k g) -> p l k g", l=2, k=K)
        reraw_flat = sb("reraw", 2 * K * NE)
        reraw = reraw_flat[:, :].rearrange("p (l g k e) -> p l g k e", l=2, g=G, k=K)
        att_out = reraw_flat[:, :].rearrange("p (j t) -> p j t", j=2)
        rw = sb("rw", 2 * K * (G + NE))[:, :].rearrange("p (l k e) -> p l k e", l=2, k=K)
        junk = sb("junk", 16)
        ssq = sb("ssq", TT)
        rstd = sb("rstd", TT)
        ssv = sb("ssv", TT * NH)
        rsv = sb("rsv", TT * NH)
        pos = sb("pos", TT * (NE + 1))
        cw = sb("cw", TT * (NE + 1))
        extra = sb("extra", 2 * NE + 1, I32)
        psum = ctx.enter_context(nc.psum_tensor("psum", [P, 8, 512], F32))
        bank = [psum[:, i, :] for i in range(8)]
        GU, YB, BA, BB = bank[4], bank[5], bank[6], bank[7]

        landed = [sem(f"landed{i}") for i in range(RING)]
        gate_used, out_half = sem("gate_used"), sem("out_half")
        first_landed = [sem(f"first_landed{i}") for i in range(2)]
        early_landed = [sem(f"early_landed{i}") for i in range(2)]
        x_loaded = [sem(f"x_loaded{t}") for t in range(TT)]
        smalls_loaded = [sem(f"smalls_loaded{i}") for i in range(7)]
        final_ready = sem("final_ready")
        ws_loaded, bs_loaded, out_stored = sem("ws_loaded"), sem("bs_loaded"), sem("out_stored")
        pool_step, consts_ready = sem("pool_step"), sem("consts_ready")
        router_ready = sem("router_ready")
        dve_step, act_step = sem("dve_step"), sem("act_step")
        cols_turned, cols_ready = sem("cols_turned"), sem("cols_ready")
        x_ready = sem("x_ready")
        std_ready, rstd_ready = sem("std_ready"), sem("rstd_ready")
        hn_dve, hn_act = sem("hn_dve"), sem("hn_act")
        hi_made, lo_made = sem("hi_made"), sem("lo_made")
        w_hi, w_lo = sem("w_hi"), sem("w_lo")
        gate_made, even_hi, even_lo = sem("gate_made"), sem("even_hi"), sem("even_lo")
        mix_made, mix_hi_made, mix_lo_made = sem("mix_made"), sem("mix_hi_made"), sem("mix_lo_made")
        turned, hT_dve, hT_act = sem("turned"), sem("hT_dve"), sem("hT_act")
        q_ready, q_taken = sem("q_ready"), sem("q_taken")
        k_ready, k_taken = sem("k_ready"), sem("k_taken")
        vv_ready, vv_taken = sem("vv_ready"), sem("vv_taken")
        v_ready, v_gelu = sem("v_ready"), sem("v_gelu")
        u_ready, u_gelu = sem("u_ready"), sem("u_gelu")
        ssv_ready, stdv_ready, vn_ready = sem("ssv_ready"), sem("stdv_ready"), sem("vn_ready")
        z_ready, clip_ready, ln_ready, sp_ready = sem("z_ready"), sem("clip_ready"), sem("ln_ready"), sem("sp_ready")
        s_ready, low_ready, a_ready = sem("s_ready"), sem("low_ready"), sem("a_ready")
        av_ready, av_taken = sem("av_ready"), sem("av_taken")
        ws_turned, ws_ready = sem("ws_turned"), sem("ws_ready")
        gate_ready = sem("gate_ready")
        o_ready = sem("o_ready")
        pc_ready, pc_taken = sem("pc_ready"), sem("pc_taken")
        ph_ready, y_made = sem("ph_ready"), sem("y_made")
        pb_ready = sem("pb_ready")
        logits_ready, tops_ready, exps_ready = sem("logits_ready"), sem("tops_ready"), sem("exps_ready")
        chosen_ready, rank_ready, extra_ready = sem("chosen_ready"), sem("rank_ready"), sem("extra_ready")
        sel_ready, gathered, xg_ready = sem("sel_ready"), sem("gathered"), sem("xg_ready")
        wsel_ready, cmb_turned, cmb_ready = sem("wsel_ready"), sem("cmb_turned"), sem("cmb_ready")
        gu_ready, silu_ready, h_ready = sem("gu_ready"), sem("silu_ready"), sem("h_ready")
        h_turned, hhT_ready, y_ready, yy_ready = sem("h_turned"), sem("hhT_ready"), sem("y_ready"), sem("yy_ready")
        xs = [{n: sem(f"x{n}{l}") for n in (
            "landed", "gate", "sel", "gathered", "xg", "gu", "silu", "h", "turned", "evac", "y", "yy", "done")}
            for l in range(2)]

        block = ctx.enter_context(nc.Block())

        def slot(n):
            return ring[:, (n % RING) * SLOT:(n % RING + 1) * SLOT]

        def wide(n):
            return slot(n).rearrange("p (k f) -> p k f", k=K)

        def tall(n):
            return slot(n).rearrange("p (j d) -> p j d", j=4)

        def lo_slot(n):
            return slot_halves[n % RING][:, :]

        def hi_slot(n):
            return lo_slot(n - LAG)

        def used_up(n):
            for l in range(2):
                if L_MOE[l] <= n < L_MOE[l] + PER_MOE:
                    n -= L_MOE[l]
                    if n >= 3 * EARLY:
                        n += 2
                    e, mat = divmod(n, 3)
                    return (gate_used, gu_ready, y_ready)[mat], after(l, e)
            if n < L_MOE[0]:
                return ((q_ready, 2), (k_ready, 2), (vv_ready, 2), (v_ready, 2), (u_ready, 2),
                        (out_half, 1), (o_ready, TT))[n - L_EVEN]
            return ((pc_ready, 2), (ph_ready, 2), (pb_ready, 2), (pc_ready, 4), (ph_ready, 4), (pb_ready, 4),
                    (out_half, 2), (o_ready, 2 * TT + 1))[n - L_ODD]

        def is_split(n):
            return L_EVEN <= n < L_MOE[0] or L_ODD <= n < L_MOE[1]

        def split_number(n):
            return n - L_EVEN if n < L_MOE[0] else L_MOE[0] - L_EVEN + n - L_ODD

        def wait_landed(eng, n, turns=0):
            eng.wait_ge(landed[n % RING], (turns + (n // RING + (n % RING > 0))) * 16)

        @contextmanager
        def further(eng):
            total = eng.value_load(extra[0:1, 2 * NE:2 * NE + 1], min_val=0, max_val=MAX_TOTAL)

            @contextmanager
            def each():
                with eng.Fori(0, NE) as e:
                    blocks = eng.value_load(extra[0:1, bass.ds(e, 1)], min_val=0, max_val=MAX_MORE)
                    before = eng.value_load(extra[0:1, bass.ds(e + NE, 1)], min_val=0, max_val=MAX_TOTAL)
                    with eng.If(blocks > 0):
                        with eng.Fori(0, blocks) as r:
                            yield e, r, before + r + 1
                    eng.nop()

            each.total = total
            with eng.If(total > 0):
                yield each
            eng.nop()

        def after(l, e):
            return e + (NE * l + 1)

        def rest_entry(l, e):
            return L_MOE[l] + 3 * e - 2


        def after_z(l, e):
            return e + ((NE + 1) * l + 2)

        def after_chunk(l, T, q):
            return T * CHUNKS + (CHUNKS * TRIS * l + q + 1)

        @block.sync
        def _(sp):
            def load(n, src, dst):
                sp.dma_start(dst, src).then_inc(landed[n % RING], 16)

            def fill(n, src, dst):
                former = n - RING
                if is_split(former + LAG):
                    former += LAG
                if former >= 0:
                    sp.wait_ge(*used_up(former))
                load(n, src, dst)

            def cols(w, c):
                return w[:, c * 512:(c + 1) * 512].rearrange("(p k) f -> p k f", k=K)

            def outrows(w, r):
                return w[r * 512:(r + 1) * 512, :].rearrange("(j p) d -> p j d", p=P)

            def load_early(l, i):
                w = (w_gate, w_up)[i][l, EARLY].rearrange("(p k) f -> p k f", k=K)
                for half in range(2):
                    sp.dma_start(early[i][half].rearrange("p (k f) -> p k f", k=HK),
                                 w[:, HK * half:HK * (half + 1), :]).then_inc(early_landed[i], 16)

            def expert(l, b, i):
                e = b * TRI + i
                for mat, (w, used) in enumerate(((w_gate, gate_used), (w_up, gu_ready), (w_down, y_ready))):
                    n = L_MOE[l] + 3 * i + mat
                    src = w[l, e].rearrange("(j p) d -> p j d", p=P) if mat == 2 else \
                        w[l, e].rearrange("(p k) f -> p k f", k=K)
                    dst = tall(n) if mat == 2 else wide(n)
                    if isinstance(b, int):
                        if (l, i, mat) == (0, TRI - 1, 1):
                            sp.wait_ge(even_lo, 6)
                            load_early(l, 0)
                        fill(n, src, dst)
                    else:
                        sp.wait_ge(used, after(l, e - TRI) if mat == 0 else after(l, e - TRI))
                        load(n, src, dst)

            def experts(l):
                for i in range(TRI):
                    expert(l, 0, i)
                if l == 1:
                    sp.wait_ge(o_ready, 2 * TT + 1)
                    load_early(l, 0)
                sp.wait_ge(logits_ready, l + 1)
                load_early(l, 1)
                with sp.Fori(1, TURNS) as b:
                    for i in range(TRI):
                        expert(l, b, i)
                for e in range(EARLY, NE):
                    n = rest_entry(l, e)
                    if e != EARLY:
                        fill(n, w_gate[l, e].rearrange("(p k) f -> p k f", k=K), wide(n))
                        fill(n + 1, w_up[l, e].rearrange("(p k) f -> p k f", k=K), wide(n + 1))
                    fill(n + 2, w_down[l, e].rearrange("(j p) d -> p j d", p=P), tall(n + 2))
                X = xs[l]
                sp.wait_ge(extra_ready, l + 1)
                with further(sp) as each:
                    with each() as (e, r, n):
                        for mat, w in enumerate((w_gate, w_up, w_down)):
                            sp.wait_ge(X[("done", "gate", "gu")[mat]], n)
                            if mat < 2:
                                src = w[l, e].rearrange("(p k) f -> p k f", k=K)
                                dst = xb.rearrange("p (k f) -> p k f", k=K)
                            else:
                                src = w[l, e].rearrange("(j p) d -> p j d", p=P)
                                dst = xb.rearrange("p (j d) -> p j d", j=4)
                            sp.dma_start(dst, src).then_inc(X["landed"], 16)

            def small_loads():
                sp.dma_start(rows[0:24, :], odd_conv_w[0].rearrange("c (j p) -> (c j) p", p=P)).then_inc(smalls_loaded[2], 16)
                sp.dma_start(rows[24:28, :], gmlp_v_gain[0].rearrange("(j a) d -> j (a d)", a=2)).then_inc(smalls_loaded[3], 16)
                for l in range(2):
                    sp.dma_start(rgraw[:, l], router_group[l].rearrange("(p k) g -> p k g", k=K)).then_inc(smalls_loaded[5], 16)
                    sp.dma_start(reraw[:, l], router_expert[l].rearrange("g (p k) e -> p g k e", k=K)).then_inc(smalls_loaded[6], 16)

            for t in range(TT):
                sp.dma_start(x[:, t, :], x_in[0, t * P:(t + 1) * P, :]).then_inc(x_loaded[t], 16)
            sp.dma_start(gains[:, 0:4:2, :], norm_mix.rearrange("n (p k) -> p n k", k=K)).then_inc(smalls_loaded[0], 16)
            sp.dma_start(gains[:, 1:4:2, :], norm_ffn.rearrange("n (p k) -> p n k", k=K)).then_inc(smalls_loaded[1], 16)
            for n, c in enumerate((2, 3, 4, 1, 0)):
                if n == 0:
                    for half in range(2):
                        ks = slice(HK * half, HK * (half + 1))
                        sp.dma_start(wide(L_EVEN)[:, ks, :], cols(even_w_in[0], c)[:, ks, :]).then_inc(first_landed[half], 16)
                    small_loads()
                else:
                    fill(L_EVEN + n, cols(even_w_in[0], c), wide(L_EVEN + n))
            for r in range(2):
                fill(L_EVEN + 5 + r, outrows(even_w_out[0], r), tall(L_EVEN + 5 + r))
            experts(0)
            for n, c in enumerate((2, 4, 0, 3, 5, 1)):
                fill(L_ODD + n, cols(odd_w_in[0], c), wide(L_ODD + n))
            for r in range(2):
                fill(L_ODD + 6 + r, outrows(odd_w_out[0], r), tall(L_ODD + 6 + r))
            experts(1)
            fill(L_GAIN, norm_final.partition_broadcast(P), slot(L_GAIN)[:, 0:D])
            for t in range(TT):
                sp.wait_ge(final_ready, t + 1)
                sp.dma_start(out[0, t * P:(t + 1) * P, :], fin[:, t, :]).then_inc(out_stored, 16)
            sp.wait_ge(out_stored, 16 * TT)

        @block.gpsimd
        def _(pool):
            steps = [0]

            def link(ins):
                steps[0] += 1
                ins.then_inc(pool_step, 1)
                pool.wait_ge(pool_step, steps[0])

            def ramp(t, base, step, chan, op, fill):
                link(pool.affine_select(out=t[:, :], in_=t[:, :], compare_op=op, fill=fill, base=base,
                                        pattern=[[step, P]], channel_multiplier=chan))

            pool.memset(eps[:, :], EPS)
            pool.memset(ones[:, :], 1.0)
            pool.memset(nones[:, :], -1.0)
            pool.memset(nlin[:, :], -1.0)
            pool.memset(ident[:, :], 0.0)
            pool.memset(below[:, :], 1.0)
            pool.memset(upto[:, :], 1.0)
            pool.memset(diag[:, :], 0.0)
            link(pool.memset(cw[:, :], 0.0))
            ramp(ident, 0, -1, 1, ALU.not_equal, 1.0)
            ramp(below, 0, 1, -1, ALU.is_gt, 0.0)
            ramp(upto, 0, 1, -1, ALU.is_ge, 0.0)
            ramp(diag, 0, 1, -1, ALU.is_gt, -BIG)
            ramp(nlin, 0, -1, 1, ALU.is_ge, 0.0)
            pool.iota(count[:, :], [[1, S]], base=0, channel_multiplier=0, allow_small_or_imprecise_dtypes=True)
            pool.memset(pos[:, :], -1.0)
            link(pool.iota(rank32[:, :], [[-1, NE]], base=NE, channel_multiplier=0,
                           allow_small_or_imprecise_dtypes=True))
            pool.sem_inc(consts_ready, 1)
            for i in (5, 6):
                pool.wait_ge(smalls_loaded[i], 32)
            for l in range(2):
                pool.tensor_copy(rw[:, l, :, 0:G], rgraw[:, l])
                for g in range(G):
                    last = pool.tensor_copy(rw[:, l, :, G + EG * g:G + EG * (g + 1)], reraw[:, l, g])
            last.then_inc(router_ready, 1)

        @block.scalar
        def _(act):
            steps = [0]

            def link(ins):
                steps[0] += 1
                ins.then_inc(act_step, 1)
                act.wait_ge(act_step, steps[0])

            act.wait_ge(consts_ready, 1)

            preloads = [0]

            def preload(func):
                act.activation(junk[:, preloads[0]:preloads[0] + 1], eps[:, 0:1], func)
                preloads[0] += 1

            def weight_hi(n, half):
                c = slice(SLOT // 2 * half, SLOT // 2 * (half + 1))
                if n == L_EVEN:
                    act.wait_ge(first_landed[half], 16)
                else:
                    wait_landed(act, n)
                if n >= LAG:
                    act.wait_ge(*used_up(n - LAG))
                act.activation(hi_slot(n)[:, c], slot(n)[:, c], ACT.Copy).then_inc(w_hi, 1)

            def roots(n):
                preload(ACT.Sqrt)
                for t in range(TT):
                    if n == 0:
                        act.wait_ge(x_loaded[t], 16)
                    else:
                        act.wait_ge(x_ready, TT * (n - 1) + t + 1)
                    link(act.activation(m[:, 0:D], x[:, t, :], ACT.Square, accum_out=ssq[:, t:t + 1]))
                    act.activation(ssq[:, t:t + 1], ssq[:, t:t + 1], ACT.Sqrt, bias=eps[:, 0:1],
                                   scale=1.0 / D).then_inc(std_ready, 1)

            def norm(n):
                if n == 2:
                    weight_hi(L_ODD, 0)
                roots(n)
                if n == 2:
                    weight_hi(L_ODD, 1)
                act.wait_ge(rstd_ready, TT * (n + 1))
                act.activation(hn[:, 1, HK:].rearrange("p k q -> p q k"),
                               x[:, 1, :].rearrange("p (q k) -> p q k", k=K)[:, :, HK:],
                               ACT.Copy, scale=rstd[:, 1:2]).then_inc(hn_act, 1)
                if n == 0:
                    act.wait_ge(smalls_loaded[0], 16)
                    act.wait_ge(smalls_loaded[1], 16)
                    weight_hi(L_EVEN, 0)
                if n % 2 == 0:
                    for j in range(4):
                        act.wait_ge(turned, 4 * n + j + 1)
                        for kk in range(2):
                            k = 2 * j + kk
                            last = act.activation(hT_hi[:, k, :], bank[4 + j][:, kk * S:(kk + 1) * S], ACT.Copy,
                                                  scale=gains[:, n, k:k + 1])
                        last.then_inc(hi_made, 1)
                    if n == 0:
                        weight_hi(L_EVEN, 1)
                    return
                for j in (1, 3):
                    act.wait_ge(turned, 4 * n + j + 1)
                    for kk in range(2):
                        k = 2 * j + kk
                        last = act.activation(hT[:, k, :], bank[4 + j][:, kk * S:(kk + 1) * S], ACT.Copy,
                                              scale=gains[:, n, k:k + 1])
                    last.then_inc(hT_act, 1)
                preload(ACT.Exp)

            def even():
                L = L_EVEN

                def hi(i):
                    for half in range(2):
                        weight_hi(L + i, half)

                hi(1)
                for j in range(2):
                    act.wait_ge(q_ready, j + 1)
                    act.activation(qT[:, 2 * j:2 * j + 2, :], bank[j][:, :].rearrange("p (j t) -> p j t", j=2),
                                   ACT.Copy, scale=HD ** -0.5).then_inc(q_taken, 1)
                hi(2)
                hi(3)

                def logs(h0):
                    for h in range(h0, h0 + 4):
                        act.wait_ge(clip_ready, h + 1)
                        ins = act.activation(att[h % 4], att[h % 4], ACT.Exp)
                        if h < h0 + 3:
                            link(ins)
                    link(ins)
                    for h in range(h0, h0 + 4):
                        act.activation(att[h % 4], att[h % 4], ACT.Ln, bias=1.0).then_inc(ln_ready, 1)

                def weights(h0):
                    for h in range(h0, h0 + 4):
                        blk = att[h % 4].rearrange("p (b t) -> p b t", b=3)
                        act.wait_ge(low_ready, h + 1)
                        act.activation(blk[:, 0:3:2, :], blk[:, 0:3:2, :], ACT.Exp)
                        act.activation(att[h % 4][:, P:2 * P], bank[h % 4][:, P:2 * P], ACT.Exp).then_inc(a_ready, 1)

                logs(0)
                hi(4)
                weights(0)
                for t in range(TT):
                    act.wait_ge(v_ready, t + 1)
                    act.activation(v[:, t, :], bank[6 + t][:, :], ACT.Gelu).then_inc(v_gelu, 1)
                hi(5)
                act.wait_ge(ssv_ready, 1)
                act.activation(ssv[:, :], ssv[:, :], ACT.Sqrt, bias=eps[:, 0:1], scale=1.0 / HD).then_inc(stdv_ready, 1)
                act.wait_ge(z_ready, NH)
                act.dma_start(ws, gmlp_w_s[0].rearrange("g t s -> t g s")).then_inc(ws_loaded, 16)
                for a in range(2):
                    src = gmlp_b_s[0].rearrange("(j a) t -> a j t", a=2)[a]
                    act.dma_start(bs[64 * a:64 * a + 64], src.partition_broadcast(HD)).then_inc(bs_loaded, 16)
                logs(4)
                for j in range(2):
                    act.wait_ge(u_ready, j + 1)
                    act.activation(uT[:, 2 * j:2 * j + 2, :], bank[4 + j][:, :].rearrange("p (j t) -> p j t", j=2),
                                   ACT.Gelu).then_inc(u_gelu, 1)
                weights(4)
                for j in range(4):
                    act.wait_ge(gate_made, j + 1)
                    act.activation(mix_hi[0][:, j, :], uT[:, j, :], ACT.Copy).then_inc(even_hi, 1)
                act.wait_ge(av_taken, 1)
                act.activation(mix_hi[0][:, 4:6, :], att_out, ACT.Copy).then_inc(even_hi, 1)
                act.wait_ge(av_ready, 2)
                act.activation(mix_hi[0][:, 6:8, :], bank[4][:, :].rearrange("p (j t) -> p j t", j=2),
                               ACT.Copy).then_inc(even_hi, 1)
                hi(6)

            def odd():
                L = L_ODD

                def hi(i):
                    for half in range(2):
                        weight_hi(L + i, half)

                def c_copy(s):
                    if s:
                        act.wait_ge(y_made, 2)
                    for j in range(2):
                        act.wait_ge(pc_ready, 2 * s + j + 1)
                        act.activation(cbuf[:, 2 * j:2 * j + 2, :], bank[j][:, :].rearrange("p (j t) -> p j t", j=2),
                                       ACT.Copy).then_inc(pc_taken, 1)

                def mixer_hi(s):
                    for j in range(2):
                        act.wait_ge(mix_made, 2 * s + j + 1)
                        act.activation(mix_hi[1][:, 4 * s + 2 * j:4 * s + 2 * j + 2, :], cv[:, 2 * j:2 * j + 2, :],
                                       ACT.Copy).then_inc(mix_hi_made, 1)

                hi(1)
                c_copy(0)
                hi(2)
                hi(3)
                mixer_hi(0)
                hi(4)
                c_copy(1)
                hi(5)
                hi(6)
                mixer_hi(1)
                hi(7)

            def expert(l, e):
                act.wait_ge(gu_ready, after(l, e))
                act.activation(sg, GU[:, 0:FP], ACT.Silu).then_inc(silu_ready, 1)
                act.wait_ge(cmb_turned, after(l, e))
                act.activation(cmb, BB[:, 0:S], ACT.Copy).then_inc(cmb_ready, 1)
                act.wait_ge(h_turned, after(l, e))
                act.activation(hhT, BA[:, 0:P], ACT.Copy).then_inc(hhT_ready, 1)
                act.wait_ge(y_ready, after(l, e))
                act.activation(yy, YB[:, 0:DP], ACT.Copy).then_inc(yy_ready, 1)

            def moe(l):
                act.wait_ge(tops_ready, l + 1)
                for t in range(TT):
                    act.activation(gs[:, t, :], lg[:, t, 0:G], ACT.Exp, bias=gneg[:, t:t + 1], accum_out=gsum[:, t:t + 1])
                    last = act.activation(ex[:, t, :], ml[:, t, 0:NE], ACT.Exp, bias=eneg[:, t:t + 1])
                last.then_inc(exps_ready, 1)
                preload(ACT.Silu)
                with act.Fori(0, TURNS) as b:
                    for i in range(TRI):
                        expert(l, b * TRI + i)
                for e in range(TURNS * TRI, NE):
                    expert(l, e)
                X = xs[l]
                act.wait_ge(extra_ready, l + 1)
                with further(act) as each:
                    with each() as (e, r, n):
                        act.wait_ge(X["gu"], n)
                        act.activation(sg, GU[:, 0:FP], ACT.Silu).then_inc(X["silu"], 1)
                        act.wait_ge(X["turned"], n)
                        act.activation(cmb, BB[:, 0:S], ACT.Copy)
                        act.activation(hhT, BA[:, 0:P], ACT.Copy).then_inc(X["evac"], 1)
                        act.wait_ge(X["y"], n)
                        act.activation(yy, YB[:, 0:DP], ACT.Copy).then_inc(X["yy"], 1)
                    act.wait_ge(X["done"], each.total + 1)
                    preload(ACT.Sqrt)

            norm(0)
            even()
            norm(1)
            moe(0)
            norm(2)
            odd()
            norm(3)
            moe(1)
            preload(ACT.Sqrt)
            act.wait_ge(o_ready, 2 * (TT + 1))
            for t in range(TT):
                ins = act.activation(m[:, D * t:D * (t + 1)].rearrange("p (c d) -> p c d", c=NP), psum[:, 0:NP, DP * t:DP * (t + 1)],
                                     ACT.Square, accum_out=ssq[:, t:t + 1])
            link(ins)
            act.activation(ssq[:, :], ssq[:, :], ACT.Sqrt, bias=eps[:, 0:1], scale=1.0 / D).then_inc(std_ready, 1)

        @block.vector
        def _(dve):
            steps = [0]

            def link(ins):
                steps[0] += 1
                ins.then_inc(dve_step, 1)
                dve.wait_ge(dve_step, steps[0])

            def update(n, t):
                dve.wait_ge(o_ready, (TT + 1) * ((n - 1) // 2) + (t + 1 if n % 2 else TT + 1))
                src = psum[:, 2 * t:2 * t + 2, :] if n % 2 else psum[:, 0:NP, DP * t:DP * (t + 1)]
                xt = x[:, t, :].rearrange("p (c d) -> p c d", c=2 if n % 2 else NP)
                if n % 2:
                    dve.tensor_tensor(xt, src, xt, ALU.add).then_inc(x_ready, 1)
                else:
                    dve.tensor_copy(xt, src).then_inc(x_ready, 1)

            def weight_lo(n, half):
                c = slice(SLOT // 2 * half, SLOT // 2 * (half + 1))
                dve.wait_ge(w_hi, 2 * split_number(n) + half + 1)
                dve.tensor_tensor(lo_slot(n)[:, c], slot(n)[:, c], hi_slot(n)[:, c].bitcast(F32),
                                  ALU.subtract).then_inc(w_lo, 1)

            def norm(n):
                if n == 2:
                    for t in range(TT):
                        update(n, t)
                for t in range(TT):
                    if n % 2:
                        update(n, t)
                    dve.wait_ge(std_ready, TT * n + t + 1)
                    dve.reciprocal(rstd[:, t:t + 1], ssq[:, t:t + 1]).then_inc(rstd_ready, 1)
                    dve.wait_ge(rstd_ready, TT * n + t + 1)
                    ks = slice(0, K) if t == 0 else slice(0, HK)
                    dve.tensor_scalar(hn[:, t, ks].rearrange("p k q -> p q k"),
                                      x[:, t, :].rearrange("p (q k) -> p q k", k=K)[:, :, ks],
                                      rstd[:, t:t + 1], None, ALU.mult).then_inc(hn_dve, 1)
                if n % 2 == 0:
                    weight_lo(L_EVEN if n == 0 else L_ODD, 0)
                if n == 0:
                    dve.wait_ge(smalls_loaded[0], 16)
                    dve.wait_ge(smalls_loaded[1], 16)
                    dve.wait_ge(turned, 4)
                if n % 2 == 0:
                    for j in range(4):
                        dve.wait_ge(hi_made, 2 * n + j + 1)
                        for kk in range(2):
                            k = 2 * j + kk
                            last = dve.scalar_tensor_tensor(out=hT_lo[n // 2][:, k, :], in0=bank[4 + j][:, kk * S:(kk + 1) * S],
                                                            scalar=gains[:, n, k:k + 1], in1=hT_hi[:, k, :].bitcast(F32),
                                                            op0=ALU.mult, op1=ALU.subtract)
                        last.then_inc(lo_made, 1)
                    weight_lo(L_EVEN if n == 0 else L_ODD, 1)
                    return
                for j in (0, 2):
                    dve.wait_ge(turned, 4 * n + j + 1)
                    dve.tensor_tensor(hT[:, 2 * j:2 * j + 2, :], bank[4 + j][:, :].rearrange("p (k t) -> p k t", k=2),
                                      gains[:, n, 2 * j:2 * j + 2].unsqueeze(2).to_broadcast([P, 2, S]),
                                      ALU.mult).then_inc(hT_dve, 1)

            def even():
                L = L_EVEN

                def lo(i):
                    for half in range(2):
                        weight_lo(L + i, half)

                lo(1)
                dve.wait_ge(cols_turned, 1)
                dve.tensor_copy(colsT[:, :], bank[4][:, 0:28]).then_inc(cols_ready, 1)
                lo(2)
                for j in range(2):
                    dve.wait_ge(k_ready, j + 1)
                    dve.tensor_copy(kT[:, 2 * j:2 * j + 2, :],
                                    bank[6 + j][:, :].rearrange("p (j t) -> p j t", j=2)).then_inc(k_taken, 1)

                def clip(h0):
                    for h in range(h0, h0 + 4):
                        dve.wait_ge(z_ready, h + 1)
                        dve.tensor_scalar(att[h % 4], bank[h % 4][:, 0:384], LINEAR, None, ALU.min).then_inc(clip_ready, 1)

                def softplus(h0):
                    for h in range(h0, h0 + 4):
                        dve.wait_ge(ln_ready, h + 1)
                        link(dve.tensor_tensor(att[h % 4], bank[h % 4][:, 0:384], att[h % 4], ALU.max))
                        blk = att[h % 4].rearrange("p (b t) -> p b t", b=3)[:, 0:3:2, :]
                        dve.tensor_tensor(blk, blk, below[:, :].unsqueeze(1).to_broadcast([P, 2, P]),
                                          ALU.mult).then_inc(sp_ready, 1)

                def lows(h0):
                    for h in range(h0, h0 + 4):
                        dve.wait_ge(s_ready, h + 1)
                        dve.tensor_tensor(att[h % 4].rearrange("p (b t) -> p b t", b=3)[:, 0:3:2, :],
                                          bank[h % 4][:, 0:384].rearrange("p (b t) -> p b t", b=3)[:, 0:3:2, :],
                                          diag[:, :].unsqueeze(1).to_broadcast([P, 2, P]), ALU.min).then_inc(low_ready, 1)

                clip(0)
                lo(3)
                softplus(0)
                for t in range(TT):
                    dve.wait_ge(vv_ready, t + 1)
                    dve.tensor_copy(vv[:, t, :], bank[4 + t][:, :]).then_inc(vv_taken, 1)
                lows(0)
                lo(4)
                for t in range(TT):
                    dve.wait_ge(v_gelu, t + 1)
                    link(dve.tensor_tensor(vsq, v[:, t, :], v[:, t, :], ALU.mult))
                    ins = dve.tensor_reduce(ssv[:, NH * t:NH * (t + 1)], vsq.rearrange("p (g c) -> p g c", g=NH),
                                            AX_X, ALU.add)
                    ins.then_inc(ssv_ready, 1) if t == TT - 1 else link(ins)
                dve.wait_ge(stdv_ready, 1)
                link(dve.reciprocal(rsv[:, :], ssv[:, :]))
                for t in range(TT):
                    vg = v[:, t, :].rearrange("p (g c) -> p g c", g=NH)
                    dve.tensor_tensor(vg, vg, rsv[:, NH * t:NH * (t + 1)].unsqueeze(2).to_broadcast([P, NH, HD]),
                                      ALU.mult).then_inc(vn_ready, 1)
                dve.wait_ge(av_ready, 1)
                dve.wait_ge(router_ready, 1)
                dve.tensor_copy(att_out, bank[6][:, :].rearrange("p (j t) -> p j t", j=2)).then_inc(av_taken, 1)
                clip(4)
                lo(5)
                softplus(4)
                dve.wait_ge(ws_turned, 1)
                for j in range(2):
                    dve.tensor_tensor(ws[:, 4 * j:4 * j + 4, :], bank[6 + j][:, :].rearrange("p (g t) -> p g t", g=4),
                                      upto[:, :].unsqueeze(1).to_broadcast([P, 4, P]), ALU.mult).then_inc(ws_ready, 1)
                lows(4)
                dve.wait_ge(bs_loaded, 32)
                dve.wait_ge(u_gelu, 2)
                dve.wait_ge(cols_ready, 1)

                def gated_lo(j):
                    dve.wait_ge(even_hi, j + 1)
                    dve.tensor_tensor(mix_lo[0][:, j, :], uT[:, j, :], mix_hi[0][:, j, :].bitcast(F32),
                                      ALU.subtract).then_inc(even_lo, 1)

                for j in range(4):
                    if j % 2 == 0:
                        dve.wait_ge(gate_ready, j // 2 + 1)
                    g3 = bank[6 + j // 2][:, S * (j % 2):S * (j % 2 + 1)].rearrange("p (c t) -> p c t", c=2)
                    mixed = vsq[:, S * (j % 2):S * (j % 2 + 1)]
                    link(dve.scalar_tensor_tensor(out=mixed.rearrange("p (c t) -> p c t", c=2), in0=g3,
                                                  scalar=colsT[:, 24 + j:25 + j],
                                                  in1=bs[:, j, :].unsqueeze(1).to_broadcast([P, 2, P]),
                                                  op0=ALU.mult, op1=ALU.add))
                    dve.tensor_tensor(uT[:, j, :], mixed, uT[:, j, :], ALU.mult).then_inc(gate_made, 1)
                    if j:
                        gated_lo(j - 1)
                gated_lo(3)
                dve.wait_ge(even_hi, 5)
                dve.tensor_tensor(mix_lo[0][:, 4:6, :], att_out, mix_hi[0][:, 4:6, :].bitcast(F32),
                                  ALU.subtract).then_inc(even_lo, 1)
                dve.wait_ge(even_hi, 6)
                dve.tensor_tensor(mix_lo[0][:, 6:8, :], bank[4][:, :].rearrange("p (j t) -> p j t", j=2),
                                  mix_hi[0][:, 6:8, :].bitcast(F32), ALU.subtract).then_inc(even_lo, 1)
                lo(6)

            def odd():
                L = L_ODD

                def lo(i):
                    for half in range(2):
                        weight_lo(L + i, half)

                def product(s):
                    for j in range(2):
                        dve.wait_ge(ph_ready, 2 * s + j + 1)
                        dve.wait_ge(pc_taken, 2 * s + j + 1)
                        dve.tensor_tensor(ybuf[:, 2 * j:2 * j + 2, PAD:], bank[2 + j][:, :].rearrange("p (j t) -> p j t", j=2),
                                          cbuf[:, 2 * j:2 * j + 2, :], ALU.mult).then_inc(y_made, 1)

                def conv(s):
                    dve.wait_ge(y_made, 2 * s + 2)
                    if s:
                        dve.wait_ge(mix_lo_made, 2)
                    for tap in range(CONV):
                        for j in range(4):
                            w = colsT[:, tap * K + 4 * s + j:tap * K + 4 * s + j + 1]
                            src = ybuf[:, j, tap:tap + S]
                            if tap == 0:
                                ins = dve.tensor_scalar(cv[:, j, :], src, w, None, ALU.mult)
                            else:
                                ins = dve.scalar_tensor_tensor(out=cv[:, j, :], in0=src, scalar=w, in1=cv[:, j, :],
                                                               op0=ALU.mult, op1=ALU.add)
                        link(ins)

                def gate(s):
                    for j in range(2):
                        dve.wait_ge(pb_ready, 2 * s + j + 1)
                        c2 = cv[:, 2 * j:2 * j + 2, :]
                        dve.tensor_tensor(c2, bank[4 + j][:, :].rearrange("p (j t) -> p j t", j=2), c2,
                                          ALU.mult).then_inc(mix_made, 1)

                def mixer_lo(s):
                    for j in range(2):
                        dve.wait_ge(mix_hi_made, 2 * s + j + 1)
                        rows2 = slice(4 * s + 2 * j, 4 * s + 2 * j + 2)
                        dve.tensor_tensor(mix_lo[1][:, rows2, :], cv[:, 2 * j:2 * j + 2, :], mix_hi[1][:, rows2, :].bitcast(F32),
                                          ALU.subtract).then_inc(mix_lo_made, 1)

                link(dve.memset(ybuf[:, :, 0:PAD], 0.0))
                lo(1)
                lo(2)
                product(0)
                lo(3)
                conv(0)
                gate(0)
                mixer_lo(0)
                lo(4)
                lo(5)
                product(1)
                lo(6)
                conv(1)
                gate(1)
                mixer_lo(1)
                lo(7)

            def fillers():
                for lt in (ml[:, :, NE:], pair8[:, :, 2:]):
                    ins = dve.memset(lt, -4 * BIG)
                link(ins)

            def route(l):
                dve.wait_ge(logits_ready, l + 1)
                link(dve.tensor_copy(lg, bank[4][:, 0:TT * (G + NE)].rearrange("p (t e) -> p t e", t=TT)))
                link(dve.tensor_reduce(gmax, lg[:, :, 0:G], AX_X, ALU.max))
                for t in range(TT):
                    ins = dve.scalar_tensor_tensor(out=gs[:, t, :], in0=lg[:, t, 0:G], scalar=gmax[:, t:t + 1],
                                                   in1=rank32[:, 0:G], op0=ALU.is_equal, op1=ALU.mult)
                link(ins)
                link(dve.tensor_reduce(gidx, gs, AX_X, ALU.max))
                for t in range(TT):
                    ins = dve.tensor_scalar(pen[:, t, :], rank32[:, 0:G], gidx[:, t:t + 1], -BIG,
                                            ALU.not_equal, ALU.mult)
                link(ins)
                for t in range(TT):
                    ins = dve.tensor_tensor(ml[:, t, 0:NE].rearrange("p (g e) -> p g e", g=G),
                                            lg[:, t, G:].rearrange("p (g e) -> p g e", g=G),
                                            pen[:, t, :].unsqueeze(2).to_broadcast([P, G, EG]), ALU.add)
                link(ins)
                for t in range(TT):
                    ins = dve.max(top8[:, t, :], ml[:, t, :])
                link(ins)
                link(dve.tensor_copy(pair8[:, :, 0:2], top8[:, :, 0:2]))
                for t in range(TT):
                    ins = dve.match_replace(mr[:, t, :], pair8[:, t, :], ml[:, t, :], -8 * BIG)
                link(ins)
                dve.tensor_scalar(chosen, mr[:, :, 0:NE], -6 * BIG, None, ALU.is_lt).then_inc(chosen_ready, 1)
                dve.tensor_scalar(gneg, gmax, -1.0, None, ALU.mult)
                dve.tensor_scalar(eneg, top8[:, :, 0:1].rearrange("p t o -> p (t o)"), -1.0, None,
                                  ALU.mult).then_inc(tops_ready, 1)
                pos3 = pos[:, :].rearrange("p (t e) -> p t e", t=TT)[:, :, 0:NE]
                dve.wait_ge(rank_ready, l + 1)
                link(dve.scalar_tensor_tensor(out=rk, in0=bank[5][:, 0:TT * NE].rearrange("p (t e) -> p t e", t=TT),
                                              scalar=1.0, in1=chosen, op0=ALU.add, op1=ALU.mult))
                link(dve.tensor_scalar(pos3, rk, -1.0, None, ALU.add))

            def expert_weights(l):
                dve.wait_ge(exps_ready, l + 1)
                link(dve.tensor_tensor(ex, ex, chosen, ALU.mult))
                link(dve.tensor_reduce(den, ex, AX_X, ALU.add))
                link(dve.tensor_tensor(den, den, gsum, ALU.mult))
                link(dve.reciprocal(den, den))
                link(dve.tensor_tensor(cw[:, :].rearrange("p (t e) -> p t e", t=TT)[:, :, 0:NE], ex,
                                       den.unsqueeze(2).to_broadcast([P, TT, NE]), ALU.mult))

            def more_blocks(l):
                limits = count[:, CAP:CAP * MAX_MORE + 1:CAP]
                counts = bank[5][:, TT * NE:TT * NE + NE]
                link(dve.tensor_tensor(over, counts.unsqueeze(2).to_broadcast([P, NE, MAX_MORE]),
                                       limits.unsqueeze(1).to_broadcast([P, NE, MAX_MORE]), ALU.is_gt))
                link(dve.tensor_reduce(more, over, AX_X, ALU.add))
                for buf in sums:
                    link(dve.memset(buf, 0.0))
                link(dve.tensor_copy(sums[0][:, HALO:], more))
                step, n = 1, 0
                while step < NE:
                    src, dst = sums[n % 2], sums[(n + 1) % 2]
                    link(dve.tensor_tensor(dst[:, HALO:], src[:, HALO:], src[:, HALO - step:HALO - step + NE], ALU.add))
                    step, n = 2 * step, n + 1
                total = sums[n % 2]
                link(dve.tensor_copy(extra[:, 0:NE], more))
                link(dve.tensor_tensor(extra[:, NE:2 * NE], total[:, HALO:], more, ALU.subtract))
                link(dve.tensor_copy(extra[:, 2 * NE:], total[:, HALO + NE - 1:]))
                dve.sem_inc(extra_ready, 1)

            def at(e, t):
                return (e + t * (NE + 1))

            def select(l, T):
                for i in range(TRI):
                    for t in range(TT):
                        c = at(T * TRI + i, t)
                        last = dve.tensor_scalar(sel[:, t, CAP * i:CAP * (i + 1)], count[:, 0:CAP],
                                                 pos[:, bass.ds(c, 1)], None, ALU.is_equal)
                last.then_inc(sel_ready, 1)

            def weigh(l, e):
                for t in range(TT):
                    c = at(e, t)
                    last = dve.tensor_scalar(wsel[:, t, :].rearrange("p (n c) -> p n c", n=NP),
                                             count[:, 0:CAP].unsqueeze(1).to_broadcast([P, NP, CAP]),
                                             pos[:, bass.ds(c, 1)], cw[:, bass.ds(c, 1)], ALU.is_equal, ALU.mult)
                last.then_inc(wsel_ready, 1)

            def gather(l, T):
                for q in range(CHUNKS):
                    dve.wait_ge(gathered, after_chunk(l, T, q))
                    b = (BA, BB)[q % 2]
                    dve.tensor_tensor(xg[:, KC * q:KC * (q + 1), :],
                                      b[:, 0:KC * TRI * CAP].rearrange("p (k c) -> p k c", k=KC),
                                      gains[:, 2 * l + 1, KC * q:KC * (q + 1)].unsqueeze(2).to_broadcast([P, KC, TRI * CAP]),
                                      ALU.mult).then_inc(xg_ready, 1)

            def expert(l, T, i, last_turn=False, last=False):
                e = T * TRI + i
                if i == 0 and not last_turn:
                    select(l, T + 1)
                dve.wait_ge(gu_ready, after(l, e))
                dve.wait_ge(silu_ready, after(l, e))
                dve.tensor_tensor(hh, GU[:, FP:2 * FP], sg, ALU.mult).then_inc(h_ready, 1)
                if i == TRI - 1:
                    gather(l, T + 1)
                if not last:
                    dve.wait_ge(cmb_turned, after(l, e))
                    weigh(l, e + 1)

            def moe(l):
                dve.memset(cmb, 0.0).then_inc(cmb_ready, 1)
                dve.memset(yy, 0.0).then_inc(yy_ready, 1)
                fillers()
                route(l)
                select(l, 0)
                expert_weights(l)
                weigh(l, 0)
                gather(l, 0)
                more_blocks(l)
                with dve.Fori(0, TURNS) as b:
                    for i in range(TRI):
                        expert(l, b, i)
                for e in range(TURNS * TRI, NE):
                    expert(l, e // TRI, e % TRI, last_turn=e // TRI == TRIS - 1, last=e == NE - 1)
                X = xs[l]
                with further(dve) as each:
                    with each() as (e, r, n):
                        dve.wait_ge(X["done"], n)
                        for t in range(TT):
                            c = at(e, t)
                            ranks = count[:, bass.ds((r + 1) * CAP, CAP)]
                            dve.tensor_scalar(sel[:, t, 0:CAP], ranks, pos[:, bass.ds(c, 1)], None, ALU.is_equal)
                            last = dve.tensor_scalar(wsel[:, t, :].rearrange("p (n c) -> p n c", n=NP),
                                                     ranks.unsqueeze(1).to_broadcast([P, NP, CAP]),
                                                     pos[:, bass.ds(c, 1)], cw[:, bass.ds(c, 1)], ALU.is_equal, ALU.mult)
                        last.then_inc(X["sel"], 1)
                        dve.wait_ge(X["gathered"], n)
                        dve.tensor_tensor(xg[:, :, 0:CAP], BA[:, 0:K * CAP].rearrange("p (k c) -> p k c", k=K),
                                          gains[:, 2 * l + 1, :].unsqueeze(2).to_broadcast([P, K, CAP]),
                                          ALU.mult).then_inc(X["xg"], 1)
                        dve.wait_ge(X["gu"], n)
                        dve.wait_ge(X["silu"], n)
                        dve.tensor_tensor(hh, GU[:, FP:2 * FP], sg, ALU.mult).then_inc(X["h"], 1)
                    dve.wait_ge(X["done"], each.total + 1)
                    dve.tensor_copy(more[:, 0:1], more[:, 0:1])

            dve.wait_ge(consts_ready, 1)
            for t in range(TT):
                dve.wait_ge(x_loaded[t], 16)
            norm(0)
            even()
            norm(1)
            moe(0)
            norm(2)
            odd()
            norm(3)
            moe(1)
            dve.wait_ge(std_ready, 4 * TT + 1)
            link(dve.reciprocal(rstd[:, :], ssq[:, :]))
            wait_landed(dve, L_GAIN)
            for t in range(TT):
                dve.scalar_tensor_tensor(out=fin[:, t, :].rearrange("p (c d) -> p c d", c=NP),
                                         in0=psum[:, 0:NP, DP * t:DP * (t + 1)], scalar=rstd[:, t:t + 1],
                                         in1=slot(L_GAIN)[:, 0:D].rearrange("p (c d) -> p c d", c=NP),
                                         op0=ALU.mult, op1=ALU.mult).then_inc(final_ready, 1)

        @block.tensor
        def _(pe):
            def norm(n):
                def turn(t):
                    for j in range(4):
                        for kk in range(2):
                            last = pe.transpose(bank[4 + j][:, kk * S + t * P:kk * S + (t + 1) * P],
                                                hn[:, t, 2 * j + kk, :], ident[:, :])
                        if t:
                            last.then_inc(turned, 1)

                pe.wait_ge(hn_dve, TT * n + 1)
                turn(0)
                if n % 2:
                    pe.wait_ge(x_ready, TT * n)
                    for t in range(TT):
                        for part in range(NP):
                            pe.matmul(bank[part][:, DP * t:DP * (t + 1)], ident[:, :], x[:, t, DP * part:DP * (part + 1)],
                                      start=t == 0, stop=False, skip_group_check=True)
                pe.wait_ge(hn_dve, TT * n + 2)
                pe.wait_ge(hn_act, n + 1)
                turn(1)

            def wait_hT(n, k):
                if k % 2 == 0:
                    pe.wait_ge((hT_dve, hT_act)[k // 2 % 2], n - 1 + k // 4 + 1)

            PAIRS = ((0, 0), (0, 1), (1, 0))

            def halves(n, **dims):
                form = "p (k f) -> p k f" if "k" in dims else "p (j d) -> p j d"
                return [w.rearrange(form, **dims) for w in (hi_slot(n), lo_slot(n))]

            def channels(n, banks, ready):
                l = int(n >= L_ODD)
                first = n in (L_EVEN, L_ODD)
                w, h = halves(n, k=K), (hT_hi, hT_lo[l])
                if not first:
                    pe.wait_ge(w_lo, 2 * split_number(n) + 2)
                for ks in ((range(HK), range(HK, K)) if first else (range(K),)):
                    if first:
                        pe.wait_ge(w_lo, 2 * split_number(n) + ks[0] // HK + 1)
                    for c in range(4):
                        for k in ks:
                            if first and c == 0 and k % 2 == 0:
                                pe.wait_ge(lo_made, 4 * l + k // 2 + 1)
                            for a, b in PAIRS:
                                last = pe.matmul(bank[banks[c // 2]][:, (c % 2) * S:(c % 2 + 1) * S],
                                                 w[a][:, k, P * c:P * (c + 1)], h[b][:, k, :],
                                                 start=k == 0 and a + b == 0 and not (first and c % 2),
                                                 stop=k == K - 1 and a == 1, skip_group_check=first)
                        if c % 2 and k == K - 1:
                            last.then_inc(ready, 1)

            def tokens(n, banks, ready):
                w, h = halves(n, k=K), (hT_hi, hT_lo[0])
                pe.wait_ge(w_lo, 2 * split_number(n) + 2)
                for t in range(TT):
                    for k in range(K):
                        for a, b in PAIRS:
                            last = pe.matmul(bank[banks[t]][:, :], h[a][:, k, P * t:P * (t + 1)], w[b][:, k, :],
                                             start=k == 0 and a + b == 0, stop=k == K - 1 and a == 1)
                    last.then_inc(ready, 1)

            def project_out(n, l, wait_rows):
                mix = (mix_hi[l], mix_lo[l])
                for r in range(2):
                    w = halves(n + r, j=4)
                    pe.wait_ge(w_lo, 2 * split_number(n + r) + 2)
                    order = [(j, t) for j in range(4) for t in range(TT)] if r == 0 else \
                        [(j, t) for t in range(TT) for j in range(4)]
                    for j, t in order:
                        if t == 0:
                            wait_rows(4 * r + j)
                        for c in range(2):
                            for a, b in PAIRS:
                                last = pe.matmul(bank[2 * t + c][:, :], mix[a][:, 4 * r + j, P * t:P * (t + 1)],
                                                 w[b][:, j, 512 * c:512 * (c + 1)],
                                                 start=r == 0 and j == 0 and a + b == 0,
                                                 stop=r == 1 and j == 3 and a == 1)
                        if r == 1 and j == 3:
                            last.then_inc(o_ready, 1)
                    if r == 0:
                        last.then_inc(out_half, 1)

            def even():
                L = L_EVEN
                channels(L, (0, 1), q_ready)
                pe.wait_ge(smalls_loaded[2], 16)
                pe.wait_ge(smalls_loaded[3], 16)
                pe.transpose(bank[4][:, 0:28], rows[:, :], ident[0:28, 0:28]).then_inc(cols_turned, 1)
                channels(L + 1, (6, 7), k_ready)

                def scores(h0):
                    for h in range(h0, h0 + 4, 2):
                        for keys in range(2):
                            for one in (h, h + 1):
                                r, c = slice(HD * (one % 2), HD * (one % 2 + 1)), one // 2
                                b = bank[one % 4]
                                lo = P * keys
                                last = pe.matmul(b[:, S * keys:S * keys + S - lo], kT[r, c, lo:lo + P], qT[r, c, lo:S],
                                                 start=keys == 0, stop=False, skip_group_check=True)
                                if keys:
                                    last.then_inc(z_ready, 1)

                def suffixes(h):
                    a, b = att[h % 4], bank[h % 4]
                    pe.wait_ge(sp_ready, h + 1)
                    pe.matmul(b[:, 0:S], nlin[:, :], a[:, 0:S], start=False, stop=False, skip_group_check=True)
                    pe.matmul(b[:, P:S], nones[:, :], a[:, S:S + P], start=False, stop=False, skip_group_check=True)
                    pe.matmul(b[:, S:S + P], nlin[:, :], a[:, S:S + P], start=False, stop=True,
                              skip_group_check=True).then_inc(s_ready, 1)

                def values(h0, b):
                    for h in range(h0, h0 + 4, 2):
                        pe.wait_ge(a_ready, h + 2)
                        for keys in range(2):
                            for one in (h, h + 1):
                                lo = P * keys
                                o = bank[b][HD * (one % 2):HD * (one % 2 + 1), S * (h % 4 // 2):S * (h % 4 // 2 + 1)]
                                last = pe.matmul(o[:, lo:S], vv[:, keys, HD * one:HD * (one + 1)],
                                                 att[one % 4][:, S * keys:S * keys + S - lo], start=keys == 0,
                                                 stop=keys == 1, skip_group_check=True)
                    last.then_inc(av_ready, 1)

                pe.wait_ge(q_taken, 2)
                pe.wait_ge(k_taken, 2)
                scores(0)
                pe.wait_ge(cols_ready, 1)
                tokens(L + 2, (4, 5), vv_ready)
                for h in range(4):
                    suffixes(h)
                tokens(L + 3, (6, 7), v_ready)
                pe.wait_ge(vv_taken, 2)
                pe.wait_ge(v_gelu, 1)
                values(0, 6)
                scores(4)
                channels(L + 4, (4, 5), u_ready)
                pe.wait_ge(ws_loaded, 16)
                pe.wait_ge(av_taken, 1)
                pe.wait_ge(v_gelu, 2)
                for g in range(NH):
                    last = pe.transpose(bank[6 + g // 4][:, P * (g % 4):P * (g % 4 + 1)], ws[:, g, :], ident[:, :])
                last.then_inc(ws_turned, 1)
                for h in range(4, 8):
                    suffixes(h)
                pe.wait_ge(ws_ready, 2)
                pe.wait_ge(vn_ready, 2)
                for j in range(4):
                    for c in range(2):
                        for g in (2 * j, 2 * j + 1):
                            last = pe.matmul(bank[6 + j // 2][HD * (g % 2):HD * (g % 2 + 1),
                                                              S * (j % 2) + P * c:S * (j % 2) + P * (c + 1)],
                                             v[:, c, HD * g:HD * (g + 1)], ws[:, g, :], start=True, stop=True)
                    if j % 2:
                        last.then_inc(gate_ready, 1)
                pe.wait_ge(u_gelu, 1)
                values(4, 4)
                project_out(L + 5, 0, lambda j: pe.wait_ge(even_lo, j + 1 if j < 4 else 4 + (j - 2) // 2))

            def odd():
                L = L_ODD
                for s in range(2):
                    if s:
                        pe.wait_ge(pc_taken, 2)
                    channels(L + 3 * s, (0, 1), pc_ready)
                    if s:
                        pe.wait_ge(y_made, 2)
                    channels(L + 3 * s + 1, (2, 3), ph_ready)
                    if s:
                        pe.wait_ge(mix_made, 2)
                    channels(L + 3 * s + 2, (4, 5), pb_ready)
                pe.wait_ge(y_made, 4)
                project_out(L + 6, 1, lambda j: pe.wait_ge(mix_lo_made, j // 2 + 1))

            def gate_up(w_of, block_of, lo):
                for k in range(K):
                    for part in range(NP):
                        last = pe.matmul(GU[CAP * part:CAP * (part + 1), lo:lo + FP], block_of(k),
                                         w_of(k)[:, FP * part:FP * (part + 1)], start=k == 0, stop=k == K - 1)
                return last

            def down(w):
                for f in range(NP):
                    for part in range(NP):
                        last = pe.matmul(YB[CAP * part:CAP * (part + 1), 0:DP], hhT[:, CAP * f:CAP * (f + 1)],
                                         w[:, f, DP * part:DP * (part + 1)], start=f == 0, stop=f == NP - 1)
                return last

            def scatter():
                for t in range(TT):
                    for part in range(NP):
                        r = slice(CAP * part, CAP * (part + 1))
                        last = pe.matmul(bank[part][:, DP * t:DP * (t + 1)], cmb[r, P * t:P * (t + 1)], yy[r, :],
                                         start=False, stop=False, skip_group_check=True)
                return last

            def turn_wsel():
                for t in range(TT):
                    last = pe.transpose(BB[:, P * t:P * (t + 1)], wsel[:, t, :], ident[:, :])
                return last

            def turn_h():
                return pe.transpose(BA[:, 0:P], hh, ident[:, :])

            def gather(l, T):
                pe.wait_ge(sel_ready, T + (TRIS * l + 1))
                for q in range(CHUNKS):
                    if q >= 2:
                        pe.wait_ge(xg_ready, after_chunk(l, T, q - 2))
                    b = (BA, BB)[q % 2]
                    for kk in range(KC):
                        for t in range(TT):
                            last = pe.matmul(b[:, kk * TRI * CAP:(kk + 1) * TRI * CAP], hn[:, t, KC * q + kk, :],
                                             sel[:, t, :], start=t == 0, stop=t == TT - 1)
                    last.then_inc(gathered, 1)

            def expert(l, T, i, rest=False):
                e = T * TRI + i
                n, turns = (rest_entry(l, e), 0) if rest else (L_MOE[l] + 3 * i, T)
                block_of = lambda k: xg[:, k, CAP * i:CAP * (i + 1)]
                for mat, used in enumerate((gate_used, gu_ready)):
                    if rest and e == EARLY:
                        pe.wait_ge(early_landed[mat], 32 * (l + 1))
                        halves = [w.rearrange("p (k f) -> p k f", k=HK) for w in early[mat]]
                        w_of = lambda k: halves[k // HK][:, k % HK, :]
                    else:
                        wait_landed(pe, n + mat, turns)
                        w_of = lambda k: wide(n + mat)[:, k, :]
                    gate_up(w_of, block_of, FP * mat).then_inc(used, 1)
                    if mat == (0 if rest and e == NE - 1 else 1):
                        pe.wait_ge(yy_ready, after_z(l, e - 1))
                        pe.wait_ge(cmb_ready, after_z(l, e - 1))
                        scatter()
                        pe.wait_ge(wsel_ready, after(l, e))
                        turn_wsel().then_inc(cmb_turned, 1)
                if i == TRI - 1:
                    pe.wait_ge(cmb_ready, after_z(l, e))
                    gather(l, T + 1)
                    pe.wait_ge(xg_ready, after_chunk(l, T + 1, 0))
                pe.wait_ge(h_ready, after(l, e))
                turn_h().then_inc(h_turned, 1)
                pe.wait_ge(hhT_ready, after(l, e))
                wait_landed(pe, n + 2, turns)
                down(tall(n + 2)).then_inc(y_ready, 1)
                if i == TRI - 1:
                    pe.wait_ge(xg_ready, after_chunk(l, T + 1, CHUNKS - 1))

            def moe(l):
                pe.wait_ge(router_ready, 1)
                for t in range(TT):
                    for k in range(K):
                        if t == 0:
                            wait_hT(2 * l + 1, k)
                        last = pe.matmul(bank[4][:, (G + NE) * t:(G + NE) * (t + 1)], hT[:, k, P * t:P * (t + 1)],
                                         rw[:, l, k, :], start=k == 0, stop=k == K - 1)
                last.then_inc(logits_ready, 1)
                pe.wait_ge(chosen_ready, l + 1)
                b = bank[5]
                pe.matmul(b[:, 0:NE], below[:, :], chosen[:, 0, :], start=True, stop=True)
                pe.matmul(b[:, NE:2 * NE], ones[:, :], chosen[:, 0, :], start=True, stop=False)
                pe.matmul(b[:, NE:2 * NE], below[:, :], chosen[:, 1, :], start=False, stop=True)
                for t in range(TT):
                    last = pe.matmul(b[:, 2 * NE:3 * NE], ones[:, :], chosen[:, t, :], start=t == 0, stop=t == TT - 1)
                last.then_inc(rank_ready, 1)
                gather(l, 0)
                pe.wait_ge(xg_ready, after_chunk(l, 0, CHUNKS - 1))
                with pe.Fori(0, TURNS) as T:
                    for i in range(TRI):
                        expert(l, T, i)
                for e in range(TURNS * TRI, NE):
                    expert(l, e // TRI, e % TRI, rest=True)
                pe.wait_ge(yy_ready, after_z(l, NE - 1))
                pe.wait_ge(cmb_ready, after_z(l, NE - 1))
                X = xs[l]
                scatter().then_inc(o_ready, 1)
                pe.wait_ge(extra_ready, l + 1)
                with further(pe) as each:
                    xw, xt = xb.rearrange("p (k f) -> p k f", k=K), xb.rearrange("p (j d) -> p j d", j=4)
                    pe.sem_inc(X["done"], 1)
                    with each() as (e, r, n):
                        pe.wait_ge(X["sel"], n)
                        for k in range(K):
                            for t in range(TT):
                                last = pe.matmul(BA[:, CAP * k:CAP * (k + 1)], hn[:, t, k, :], sel[:, t, 0:CAP],
                                                 start=t == 0, stop=t == TT - 1)
                        last.then_inc(X["gathered"], 1)
                        pe.wait_ge(X["xg"], n)
                        for mat in range(2):
                            pe.wait_ge(X["landed"], n * 48 - 16 * (2 - mat))
                            gate_up(lambda k: xw[:, k, :], lambda k: xg[:, k, 0:CAP], FP * mat).then_inc(X[("gate", "gu")[mat]], 1)
                        turn_wsel()
                        pe.wait_ge(X["h"], n)
                        turn_h().then_inc(X["turned"], 1)
                        pe.wait_ge(X["evac"], n)
                        pe.wait_ge(X["landed"], n * 48)
                        down(xt).then_inc(X["y"], 1)
                        pe.wait_ge(X["yy"], n)
                        scatter().then_inc(X["done"], 1)

            pe.wait_ge(consts_ready, 1)
            norm(0)
            even()
            norm(1)
            moe(0)
            norm(2)
            odd()
            norm(3)
            moe(1)


NAMES = ("x", "even_w_in", "even_w_out", "gmlp_w_s", "gmlp_b_s", "gmlp_v_gain", "odd_w_in", "odd_conv_w",
         "odd_w_out", "norm_mix", "norm_ffn", "router_group", "router_expert", "w_gate", "w_up", "w_down",
         "norm_final")


def kernel(**inputs):
    import numpy as np
    import concourse.bacc as bacc
    from concourse.bass_utils import run_bass_kernel_spmd

    nc = bacc.Bacc("TRN2", target_bir_lowering=False, num_devices=1)
    arrays, args = {}, []
    for name in NAMES:
        a = np.ascontiguousarray(inputs[name])
        arrays[f"in_{name}"] = a
        args.append(nc.dram_tensor(f"in_{name}", a.shape, mybir.dt.from_np(a.dtype), kind="ExternalInput").ap())
    args.append(nc.dram_tensor("out", (1, S, D), F32, kind="ExternalOutput").ap())
    trunk(nc, *args)
    return run_bass_kernel_spmd(nc, [arrays], core_ids=[0]).results[0]["out"]
```
